# Optimizing a Trainium2 kernel written in Bass

```python
import math
import jax, jax.numpy as jnp
from jax import lax
import numpy as np

D_MODEL = 1024
BATCH = 1
SEQ = 512
DEPTH = 2

N_MIXERS = 4
DN_ALPHA = (2.0 * DEPTH) ** 0.25
DN_BETA = (8.0 * DEPTH) ** -0.25
LN_EPS = 1e-5

GDN_HEADS = 8
GDN_DK = D_MODEL // GDN_HEADS
GDN_DV = D_MODEL // GDN_HEADS
GDN_CONV = 4
GDN_CHUNK = 64
RET_HEADS = 4
RET_DK = D_MODEL // RET_HEADS
RET_DV = 2 * D_MODEL // RET_HEADS
RET_CHUNK = 128
RET_ROPE_BASE = 10000.0
GMLP_CHUNK = 128
GMLP_WIDTH = 2 * D_MODEL
GMLP_GROUPS = 8
SB_HEADS = 16
SB_DH = D_MODEL // SB_HEADS
SB_BLOCK = 128
FFN_HIDDEN = ((8 * D_MODEL // 3 + 255) // 256) * 256
FFN_CONV = 3


F32 = jnp.float32

def _standardize(x, eps):
    xf = x.astype(F32)
    mu = jnp.mean(xf, axis=-1, keepdims=True)
    xc = xf - mu
    var = jnp.mean(xc * xc, axis=-1, keepdims=True)
    return xc * lax.rsqrt(var + eps)

def layer_norm(x, g, b):
    return (_standardize(x, LN_EPS) * g.astype(F32) + b.astype(F32)).astype(x.dtype)

def _l2norm(x, eps=1e-6):
    return x * lax.rsqrt(jnp.sum(x * x, axis=-1, keepdims=True) + eps)

def causal_dwconv(x, w):
    k_w = w.shape[0]
    s = x.shape[1]
    xp = jnp.pad(x, ((0, 0), (k_w - 1, 0), (0, 0)))
    y = xp[:, k_w - 1:k_w - 1 + s] * w[k_w - 1]
    for j in range(k_w - 1):
        y = y + xp[:, j:j + s] * w[j]
    return y

def _chunk_heads(t, n_heads, chunk):
    b, s, hd = t.shape
    return t.astype(F32).reshape(b, s // chunk, chunk, n_heads, hd // n_heads).transpose(0, 3, 1, 2, 4)

def _unchunk_heads(t):
    b, h, n, c, d = t.shape
    return t.transpose(0, 2, 3, 1, 4).reshape(b, n * c, h, d)

def gated_deltanet(h, w_in, conv_w, a_log, dt_bias, norm_w, w_out):
    H, dk, dv, C = GDN_HEADS, GDN_DK, GDN_DV, GDN_CHUNK
    b_, s, _ = h.shape
    n_qkv = 2 * H * dk + H * dv
    proj = h @ w_in
    qkv, z, a, bt = jnp.split(proj, [n_qkv, n_qkv + H * dv, n_qkv + H * dv + H], axis=-1)
    qkv = jax.nn.silu(causal_dwconv(qkv, conv_w))
    q, k, v = jnp.split(qkv, [H * dk, 2 * H * dk], axis=-1)
    q = _l2norm(_chunk_heads(q, H, C)) * (dk ** -0.5)
    k = _l2norm(_chunk_heads(k, H, C))
    v = _chunk_heads(v, H, C)
    beta = jax.nn.sigmoid(_chunk_heads(bt, H, C)[..., 0])
    g = -jnp.exp(a_log.astype(F32))[:, None, None] * jax.nn.softplus(
        _chunk_heads(a, H, C)[..., 0] + dt_bias.astype(F32)[:, None, None])
    gc = jnp.cumsum(g, axis=-1)
    idx = jnp.arange(C)
    causal = idx[:, None] >= idx[None, :]
    strict = idx[:, None] > idx[None, :]
    diff = gc[..., :, None] - gc[..., None, :]
    decay = jnp.where(causal, jnp.exp(jnp.where(causal, diff, 0.0)), 0.0)
    kb = k * beta[..., None]
    kk = jnp.where(strict, jnp.einsum('bhncd,bhnmd->bhncm', kb, k) * decay, 0.0)
    eye = jnp.eye(C, dtype=F32)
    rhs = jnp.concatenate([v * beta[..., None], kb * jnp.exp(gc)[..., None]], axis=-1)
    sol = lax.linalg.triangular_solve(kk + eye, rhs, left_side=True, lower=True, unit_diagonal=True)
    u, w = sol[..., :dv], sol[..., dv:]
    qk = jnp.where(causal, jnp.einsum('bhncd,bhnmd->bhncm', q, k) * decay, 0.0)

    def step(state, inp):
        q_n, k_n, u_n, w_n, qk_n, g_n = inp
        v_new = u_n - jnp.einsum('bhck,bhkv->bhcv', w_n, state)
        o = (jnp.einsum('bhck,bhkv->bhcv', q_n * jnp.exp(g_n)[..., None], state)
             + jnp.einsum('bhcm,bhmv->bhcv', qk_n, v_new))
        g_last = g_n[..., -1:]
        state = (state * jnp.exp(g_last)[..., None]
                 + jnp.einsum('bhck,bhcv->bhkv', k_n * jnp.exp(g_last - g_n)[..., None], v_new))
        return state, o

    xs = tuple(jnp.moveaxis(t, 2, 0) for t in (q, k, u, w, qk, gc))
    state0 = jnp.zeros((b_, H, dk, dv), F32)
    _, o = lax.scan(step, state0, xs)
    o = _unchunk_heads(jnp.moveaxis(o, 0, 2))
    o = o * lax.rsqrt(jnp.mean(o * o, axis=-1, keepdims=True) + 1e-6) * norm_w.astype(F32)
    o = o * jax.nn.silu(z.astype(F32).reshape(b_, s, H, dv))
    return o.reshape(b_, s, H * dv).astype(h.dtype) @ w_out

def retention(h, w_in, w_out):
    H, dk, dv, C = RET_HEADS, RET_DK, RET_DV, RET_CHUNK
    b_, s, _ = h.shape
    q, k, v, gate = jnp.split(h @ w_in, [H * dk, 2 * H * dk, 2 * H * dk + H * dv], axis=-1)
    pos = jnp.arange(s, dtype=F32)
    inv_freq = RET_ROPE_BASE ** (-jnp.linspace(0.0, 1.0, dk // 2, dtype=F32))
    ang = pos[:, None] * inv_freq[None, :]
    cos_a, sin_a = jnp.cos(ang)[:, None, :], jnp.sin(ang)[:, None, :]

    def rot(t):
        t = t.astype(F32).reshape(b_, s, H, dk)
        t1, t2 = t[..., :dk // 2], t[..., dk // 2:]
        return jnp.concatenate([t1 * cos_a - t2 * sin_a, t1 * sin_a + t2 * cos_a], axis=-1).reshape(b_, s, H * dk)

    q = _chunk_heads(rot(q), H, C)
    k = _chunk_heads(rot(k), H, C) * (dk ** -0.5)
    v = _chunk_heads(v, H, C)
    log_gamma = jnp.log(1.0 - jnp.power(2.0, -5.0 - jnp.arange(H, dtype=F32)))
    idx = jnp.arange(C, dtype=F32)
    rel = idx[:, None] - idx[None, :]
    dmask = jnp.where(rel >= 0, jnp.exp(jnp.maximum(rel, 0.0) * log_gamma[:, None, None]), 0.0)
    scores = jnp.einsum('bhncd,bhnmd->bhncm', q, k) * dmask[None, :, None]
    intra = jnp.einsum('bhncm,bhnmv->bhncv', scores, v)
    zeta = jnp.exp((C - 1.0 - idx)[None, :] * log_gamma[:, None])
    xi = jnp.exp((idx + 1.0)[None, :] * log_gamma[:, None])
    gamma_c = jnp.exp(C * log_gamma)

    def step(state, inp):
        q_n, k_n, v_n = inp
        o = jnp.einsum('bhck,bhkv->bhcv', q_n, state) * xi[None, :, :, None]
        state = (state * gamma_c[None, :, None, None]
                 + jnp.einsum('bhck,bhcv->bhkv', k_n * zeta[None, :, :, None], v_n))
        return state, o

    xs = tuple(jnp.moveaxis(t, 2, 0) for t in (q, k, v))
    _, inter = lax.scan(step, jnp.zeros((b_, H, dk, dv), F32), xs)
    o = _unchunk_heads(intra + jnp.moveaxis(inter, 0, 2))
    o = _standardize(o, 1e-6).reshape(b_, s, H * dv)
    o = o * jax.nn.silu(gate.astype(F32))
    return o.astype(h.dtype) @ w_out

def chunked_gmlp(h, w_in, ln_g, ln_b, w_s, b_s, w_out):
    C, G, W = GMLP_CHUNK, GMLP_GROUPS, GMLP_WIDTH
    b_, s, _ = h.shape
    u, v = jnp.split(jax.nn.gelu(h @ w_in, approximate=False), 2, axis=-1)
    v = layer_norm(v, ln_g, ln_b).reshape(b_, s // C, C, G, W // G)
    causal = jnp.tril(jnp.ones((C, C), dtype=bool))
    ws = jnp.where(causal, w_s, 0.0).astype(v.dtype)
    vs = jnp.einsum('gts,bnsgd->bntgd', ws, v) + b_s.T.astype(v.dtype)[None, None, :, :, None]
    return (u * vs.reshape(b_, s, W)) @ w_out

def stick_breaking(h, w_in, w_out):
    H, dh, T = SB_HEADS, SB_DH, SB_BLOCK
    b_, s, _ = h.shape
    nb = s // T
    q, k, v = jnp.split(h @ w_in, 3, axis=-1)
    q, k, v = (t.reshape(b_, s, H, dh).transpose(0, 2, 1, 3) for t in (q, k, v))
    qb = q.reshape(b_, H, nb, T, dh).transpose(2, 0, 1, 3, 4)
    key_pos = jnp.arange(s)
    scale = dh ** -0.5

    def block(args):
        q_blk, blk = args
        z = jnp.einsum('bhtd,bhsd->bhts', q_blk, k).astype(F32) * scale
        q_pos = blk * T + jnp.arange(T)
        strict = key_pos[None, :] < q_pos[:, None]
        log_1mb = jnp.where(strict, jax.nn.log_sigmoid(-z), 0.0)
        after = lax.cumsum(log_1mb, axis=3, reverse=True) - log_1mb
        a = jnp.where(strict, jnp.exp(jax.nn.log_sigmoid(z) + after), 0.0)
        return jnp.einsum('bhts,bhsd->bhtd', a.astype(v.dtype), v)

    o = lax.map(block, (qb, jnp.arange(nb)))
    o = o.transpose(1, 0, 3, 2, 4).reshape(b_, s, H * dh)
    return o @ w_out

def conv_ffn(h, w_up, conv_w, conv_b, w_down):
    gate, up = jnp.split(h @ w_up, 2, axis=-1)
    gate = causal_dwconv(gate, conv_w) + conv_b
    return (jax.nn.silu(gate) * up) @ w_down

def first_inputs(seed: int = 0) -> dict:
    key = jax.random.key(seed)
    ks = jax.random.split(key, 32)
    D, F = D_MODEL, FFN_HIDDEN

    def nrm(i, shape, scale):
        return jax.random.normal(ks[i], shape, F32) * scale

    gdn_qkv = 2 * GDN_HEADS * GDN_DK + GDN_HEADS * GDN_DV
    gdn_in = gdn_qkv + GDN_HEADS * GDN_DV + 2 * GDN_HEADS
    ret_in = 2 * RET_HEADS * RET_DK + 2 * RET_HEADS * RET_DV
    a_vals = jax.random.uniform(ks[14], (GDN_HEADS,), F32, 1.0, 16.0)
    dt = jnp.exp(jax.random.uniform(ks[15], (GDN_HEADS,), F32, math.log(1e-3), math.log(1e-1)))
    return {
        'x': nrm(0, (BATCH, SEQ, D), 1.0),
        'c': nrm(1, (BATCH, D), 1.0),
        'cond_w': nrm(2, (D, D), D ** -0.5),
        'cond_b': nrm(3, (D,), 0.01),
        'ada_w': nrm(4, (DEPTH, D, 6 * D), 0.1 * D ** -0.5),
        'ada_b': nrm(5, (DEPTH, 6 * D), 0.01),
        'ln_g': 1.0 + nrm(6, (DEPTH, 2, D), 0.02),
        'ln_b': nrm(7, (DEPTH, 2, D), 0.02),
        'ffn_up': nrm(8, (DEPTH, D, 2 * F), D ** -0.5),
        'ffn_conv_w': nrm(9, (DEPTH, FFN_CONV, F), FFN_CONV ** -0.5),
        'ffn_conv_b': nrm(10, (DEPTH, F), 0.01),
        'ffn_down': nrm(11, (DEPTH, F, D), DN_BETA * F ** -0.5),
        'gdn_w_in': nrm(12, (D, gdn_in), D ** -0.5),
        'gdn_conv_w': nrm(13, (GDN_CONV, gdn_qkv), GDN_CONV ** -0.5),
        'gdn_a_log': jnp.log(a_vals),
        'gdn_dt_bias': dt + jnp.log(-jnp.expm1(-dt)),
        'gdn_norm_w': 1.0 + nrm(16, (GDN_DV,), 0.02),
        'gdn_w_out': nrm(17, (GDN_HEADS * GDN_DV, D), DN_BETA * (GDN_HEADS * GDN_DV) ** -0.5),
        'ret_w_in': nrm(18, (D, ret_in), D ** -0.5),
        'ret_w_out': nrm(19, (RET_HEADS * RET_DV, D), DN_BETA * (RET_HEADS * RET_DV) ** -0.5),
        'gmlp_w_in': nrm(20, (D, 2 * GMLP_WIDTH), D ** -0.5),
        'gmlp_ln_g': 1.0 + nrm(21, (GMLP_WIDTH,), 0.02),
        'gmlp_ln_b': nrm(22, (GMLP_WIDTH,), 0.02),
        'gmlp_w_s': nrm(23, (GMLP_GROUPS, GMLP_CHUNK, GMLP_CHUNK), GMLP_CHUNK ** -0.5),
        'gmlp_b_s': 1.0 + nrm(24, (GMLP_GROUPS, GMLP_CHUNK), 0.01),
        'gmlp_w_out': nrm(25, (GMLP_WIDTH, D), DN_BETA * GMLP_WIDTH ** -0.5),
        'sb_w_in': nrm(26, (D, 3 * D), D ** -0.5),
        'sb_w_out': nrm(27, (D, D), DN_BETA * D ** -0.5),
    }

def first_block(x, c, cond_w, cond_b, ada_w, ada_b, ln_g, ln_b, ffn_up, ffn_conv_w, ffn_conv_b, ffn_down,
              gdn_w_in, gdn_conv_w, gdn_a_log, gdn_dt_bias, gdn_norm_w, gdn_w_out,
              ret_w_in, ret_w_out,
              gmlp_w_in, gmlp_ln_g, gmlp_ln_b, gmlp_w_s, gmlp_b_s, gmlp_w_out,
              sb_w_in, sb_w_out):
    mixers = (
        lambda t: gated_deltanet(t, gdn_w_in, gdn_conv_w, gdn_a_log, gdn_dt_bias, gdn_norm_w, gdn_w_out),
        lambda t: retention(t, ret_w_in, ret_w_out),
        lambda t: chunked_gmlp(t, gmlp_w_in, gmlp_ln_g, gmlp_ln_b, gmlp_w_s, gmlp_b_s, gmlp_w_out),
        lambda t: stick_breaking(t, sb_w_in, sb_w_out),
    )
    e = jax.nn.silu(c @ cond_w + cond_b)
    for i in range(DEPTH):
        mod = (e @ ada_w[i] + ada_b[i])[:, None, :]
        sh1, sc1, g1, sh2, sc2, g2 = jnp.split(mod, 6, axis=-1)
        y = mixers[i % N_MIXERS](x * (1.0 + sc1) + sh1)
        x = layer_norm(DN_ALPHA * x + (1.0 + g1) * y, ln_g[i, 0], ln_b[i, 0])
        y = conv_ffn(x * (1.0 + sc2) + sh2, ffn_up[i], ffn_conv_w[i], ffn_conv_b[i], ffn_down[i])
        x = layer_norm(DN_ALPHA * x + (1.0 + g2) * y, ln_g[i, 1], ln_b[i, 1])
    return x


DEPTH_2 = 1

N_META = 16
D_MIX = D_MODEL
D_HYENA = D_MIX // 2
D_HGRN = D_MIX - D_HYENA
HYENA_ORDER = 2
SHORT_CONV = 3
FILTER_EMB = 33
FILTER_BANDS = (FILTER_EMB - 1) // 2
FILTER_HIDDEN = 64
DECAY_TARGET = 1e-2
FAST_DECAY_PCT = 0.3
SLOW_DECAY_PCT = 1.5
HGRN_HEAD_DIM = 128
HGRN_HEADS = D_HGRN // HGRN_HEAD_DIM
CHUNK = 64
N_GROUPS = 8
EXPERTS_PER_GROUP = 8
N_EXPERTS = N_GROUPS * EXPERTS_PER_GROUP
TOP_K = 2
D_EXPERT = D_MODEL // 2
MOE_BLOCK = 128
D_HYENA_PROJ = (HYENA_ORDER + 1) * D_HYENA
D_HGRN_PROJ = 5 * D_HGRN
D_IN_PROJ = D_HYENA_PROJ + D_HGRN_PROJ
EPS = 1e-6


def rms_norm(x, gain):
    xf = x.astype(jnp.float32)
    y = xf * lax.rsqrt(jnp.mean(xf * xf, axis=-1, keepdims=True) + EPS)
    return (y * gain.astype(jnp.float32)).astype(x.dtype)

def centred_short_conv(u, w, b):
    L = u.shape[1]
    half = SHORT_CONV // 2
    up = jnp.pad(u, ((0, 0), (half, SHORT_CONV - 1 - half), (0, 0)))
    y = b
    for j in range(SHORT_CONV):
        y = y + up[:, j:j + L] * w[j]
    return y

def hyena_filter_spectra(L, w1, b1, w2, b2, w3, freq):
    f32 = jnp.float32
    pos = jnp.arange(L, dtype=f32)
    t = pos / max(L - 1, 1)
    bands = jnp.linspace(1e-4, FILTER_BANDS - 1, FILTER_BANDS, dtype=f32)
    ang = (2.0 * math.pi / L) * pos[:, None] * bands[None, :]
    z = jnp.concatenate([t[:, None], jnp.cos(ang), -jnp.sin(ang)], axis=-1)
    fr = freq.astype(f32)
    hid = jnp.sin(fr * (z @ w1.astype(f32) + b1.astype(f32)))
    hid = jnp.sin(fr * (hid @ w2.astype(f32) + b2.astype(f32)))
    filt = (hid @ w3.astype(f32)).reshape(L, 2, HYENA_ORDER, D_HYENA)
    deltas = jnp.abs(jnp.linspace(math.log(DECAY_TARGET) / SLOW_DECAY_PCT,
                                  math.log(DECAY_TARGET) / FAST_DECAY_PCT, D_HYENA, dtype=f32))
    window = jnp.exp(-t[:, None] * deltas[None, :])
    filt = filt * window[:, None, None, :]
    h_fwd, h_bwd = filt[:, 0], filt[:, 1]
    two_sided = jnp.concatenate([h_fwd, jnp.zeros_like(h_fwd[:1]), h_bwd[:0:-1]], axis=0)
    return jnp.fft.rfft(two_sided, axis=0)

def fft_long_conv(u, spec, skip):
    L = u.shape[1]
    uf = u.astype(jnp.float32)
    y = jnp.fft.irfft(jnp.fft.rfft(uf, n=2 * L, axis=1) * spec[None], n=2 * L, axis=1)[:, :L]
    return (y + uf * skip.astype(jnp.float32)).astype(u.dtype)

def hyena_mixer(p, conv_w, conv_b, w1, b1, w2, b2, w3, freq, skip):
    L = p.shape[1]
    u = centred_short_conv(p, conv_w, conv_b)
    z = u[..., :D_HYENA]
    spectra = hyena_filter_spectra(L, w1, b1, w2, b2, w3, freq)
    for n in range(HYENA_ORDER):
        gate = u[..., (n + 1) * D_HYENA:(n + 2) * D_HYENA]
        z = gate * fft_long_conv(z, spectra[:, n], skip[n])
    return z

def chunked_gated_linear_scan(q, k, v, log_f):
    B, T, H, DK = q.shape
    DV = v.shape[-1]
    N = T // CHUNK
    q, k, v, log_f = [a.reshape(B, N, CHUNK, H, a.shape[-1]) for a in (q, k, v, log_f)]
    b = jnp.cumsum(log_f, axis=2)
    b_last = b[:, :, -1]
    b_mid = b[:, :, CHUNK // 2][:, :, None]
    scores = jnp.einsum('bnthd,bnshd->bnhts', q * jnp.exp(b - b_mid), k * jnp.exp(b_mid - b))
    lower_tri = jnp.tril(jnp.ones((CHUNK, CHUNK), dtype=bool))
    scores = jnp.where(lower_tri, scores, 0.0)
    o_intra = jnp.einsum('bnhts,bnshv->bnthv', scores, v)
    chunk_state = jnp.einsum('bnshd,bnshv->bnhdv', k * jnp.exp(b_last[:, :, None] - b), v)
    chunk_decay = jnp.exp(b_last)

    def step(S, inp):
        dec, U = inp
        return dec[..., None] * S + U, S

    S0 = jnp.zeros((B, H, DK, DV), q.dtype)
    _, S_in = lax.scan(step, S0, (jnp.moveaxis(chunk_decay, 1, 0), jnp.moveaxis(chunk_state, 1, 0)))
    S_in = jnp.moveaxis(S_in, 0, 1)
    o_inter = jnp.einsum('bnthd,bnhdv->bnthv', q * jnp.exp(b), S_in)
    return (o_intra + o_inter).reshape(B, T, H, DV)

def hgrn2_mixer(p, lb_f, lb_b, norm_w):
    f32 = jnp.float32
    B, L, _ = p.shape
    q, f_fwd, f_bwd, i_in, g = [p[..., j * D_HGRN:(j + 1) * D_HGRN] for j in range(5)]

    def heads(a):
        return a.reshape(B, L, HGRN_HEADS, HGRN_HEAD_DIM)

    qh = heads(jax.nn.silu(q.astype(f32)))
    vh = heads(i_in.astype(f32))

    def forget(logit, lb):
        lb = lb.astype(f32)
        f = lb + (1.0 - lb) * jax.nn.sigmoid(logit.astype(f32))
        return heads(1.0 - f), heads(jnp.log(f))

    k_f, lf_f = forget(f_fwd, lb_f)
    k_b, lf_b = forget(f_bwd, lb_b)
    n_pad = (-N_META) % CHUNK

    def pad(a):
        return jnp.pad(a, ((0, 0), (n_pad, 0), (0, 0), (0, 0)))

    def flip(a):
        return a[:, ::-1]

    qp, vp = pad(qh), pad(vh)
    o_f = chunked_gated_linear_scan(qp, pad(k_f), vp, pad(lf_f))
    o_b = flip(chunked_gated_linear_scan(flip(qp), flip(pad(k_b)), flip(vp), flip(pad(lf_b))))
    o = (o_f + o_b)[:, n_pad:]
    o = o * lax.rsqrt(jnp.mean(o * o, axis=-1, keepdims=True) + EPS)
    o = o.reshape(B, L, D_HGRN) * norm_w.astype(f32) * jax.nn.silu(g.astype(f32))
    return o.astype(p.dtype)

def hier_moe(h, w_rg, w_re, w_gate, w_up, w_down):
    f32 = jnp.float32
    B, L, D = h.shape
    n_tok = B * L
    hf = h.reshape(n_tok, D)
    g_logits = (hf @ w_rg).astype(f32)
    g_sel = jnp.argmax(g_logits, axis=-1)
    p_group = jnp.take_along_axis(jax.nn.softmax(g_logits, axis=-1), g_sel[:, None], axis=-1)
    e_logits = jnp.einsum('nd,dge->nge', hf, w_re).astype(f32)
    e_logits = e_logits[jnp.arange(n_tok), g_sel]
    p_top, e_top = lax.top_k(jax.nn.softmax(e_logits, axis=-1), TOP_K)
    gate = p_group * p_top / jnp.sum(p_top, axis=-1, keepdims=True)
    expert_id = (g_sel[:, None] * EXPERTS_PER_GROUP + e_top).reshape(-1).astype(jnp.int32)

    M = n_tok * TOP_K
    n_blocks = -(-M // MOE_BLOCK) + N_EXPERTS
    n_slots = n_blocks * MOE_BLOCK
    order = jnp.argsort(expert_id)
    eid_s = expert_id[order]
    tok_s = (jnp.arange(M, dtype=jnp.int32) // TOP_K)[order]
    gate_s = gate.reshape(-1)[order]
    counts = jnp.bincount(expert_id, length=N_EXPERTS)
    padded = (counts + MOE_BLOCK - 1) // MOE_BLOCK * MOE_BLOCK
    start = jnp.cumsum(counts) - counts
    pend = jnp.cumsum(padded)
    dest = (pend - padded)[eid_s] + jnp.arange(M, dtype=jnp.int32) - start[eid_s]
    tok_buf = jnp.zeros((n_slots,), jnp.int32).at[dest].set(tok_s)
    gate_buf = jnp.zeros((n_slots,), f32).at[dest].set(gate_s)
    block_eid = jnp.minimum(
        jnp.searchsorted(pend, jnp.arange(n_blocks, dtype=pend.dtype) * MOE_BLOCK, side='right'),
        N_EXPERTS - 1)
    xb = hf[tok_buf].reshape(n_blocks, MOE_BLOCK, D)

    def expert_block(args):
        xe, e = args
        return (jax.nn.silu(xe @ w_gate[e]) * (xe @ w_up[e])) @ w_down[e]

    yb = lax.map(expert_block, (xb, block_eid)).reshape(n_slots, D)
    y = jnp.zeros_like(hf).at[tok_buf].add(yb * gate_buf[:, None].astype(yb.dtype))
    return y.reshape(B, L, D)

def second_inputs(seed: int = 0) -> dict:
    key = jax.random.key(seed)
    ks = jax.random.split(key, 25)

    def nrm(k, shape, scale):
        return scale * jax.random.normal(k, shape, jnp.float32)

    return {
        'x': nrm(ks[0], (BATCH, SEQ, D_MODEL), 1.0),
        'meta_tokens': nrm(ks[1], (N_META, D_MODEL), 1.0),
        'w_in': nrm(ks[2], (DEPTH_2, D_MODEL, D_IN_PROJ), D_MODEL ** -0.5),
        'conv_w': nrm(ks[3], (DEPTH_2, SHORT_CONV, D_HYENA_PROJ), SHORT_CONV ** -0.5),
        'conv_b': nrm(ks[4], (DEPTH_2, D_HYENA_PROJ), 0.01),
        'filt_w1': nrm(ks[5], (DEPTH_2, FILTER_EMB, FILTER_HIDDEN), FILTER_EMB ** -0.5),
        'filt_b1': nrm(ks[6], (DEPTH_2, FILTER_HIDDEN), 0.1),
        'filt_w2': nrm(ks[7], (DEPTH_2, FILTER_HIDDEN, FILTER_HIDDEN), FILTER_HIDDEN ** -0.5),
        'filt_b2': nrm(ks[8], (DEPTH_2, FILTER_HIDDEN), 0.1),
        'filt_w3': nrm(ks[9], (DEPTH_2, FILTER_HIDDEN, 2 * HYENA_ORDER * D_HYENA), 0.02),
        'filt_freq': 1.0 + nrm(ks[10], (DEPTH_2, FILTER_HIDDEN), 0.01),
        'filt_skip': nrm(ks[11], (DEPTH_2, HYENA_ORDER, D_HYENA), 1.0),
        'hyena_norm': 1.0 + nrm(ks[12], (DEPTH_2, D_HYENA), 0.01),
        'lb_fwd': nrm(ks[13], (DEPTH_2 + 1, D_HGRN), 0.1),
        'lb_bwd': nrm(ks[14], (DEPTH_2 + 1, D_HGRN), 0.1),
        'hgrn_norm': 1.0 + nrm(ks[15], (DEPTH_2, D_HGRN), 0.01),
        'w_out': nrm(ks[16], (DEPTH_2, D_MIX, D_MODEL), D_MIX ** -0.5),
        'norm_mix': 1.0 + nrm(ks[17], (DEPTH_2, D_MODEL), 0.01),
        'norm_ffn': 1.0 + nrm(ks[18], (DEPTH_2, D_MODEL), 0.01),
        'w_router_group': nrm(ks[19], (DEPTH_2, D_MODEL, N_GROUPS), D_MODEL ** -0.5),
        'w_router_expert': nrm(ks[20], (DEPTH_2, D_MODEL, N_GROUPS, EXPERTS_PER_GROUP), D_MODEL ** -0.5),
        'w_gate': nrm(ks[21], (DEPTH_2, N_EXPERTS, D_MODEL, D_EXPERT), D_MODEL ** -0.5),
        'w_up': nrm(ks[22], (DEPTH_2, N_EXPERTS, D_MODEL, D_EXPERT), D_MODEL ** -0.5),
        'w_down': nrm(ks[23], (DEPTH_2, N_EXPERTS, D_EXPERT, D_MODEL), D_EXPERT ** -0.5),
        'norm_final': 1.0 + nrm(ks[24], (D_MODEL,), 0.01),
    }

def second_block(x, meta_tokens, w_in, conv_w, conv_b, filt_w1, filt_b1, filt_w2, filt_b2, filt_w3,
              filt_freq, filt_skip, hyena_norm, lb_fwd, lb_bwd, hgrn_norm, w_out, norm_mix, norm_ffn,
              w_router_group, w_router_expert, w_gate, w_up, w_down, norm_final):
    B = x.shape[0]
    meta = jnp.broadcast_to(meta_tokens[None].astype(x.dtype), (B, N_META, x.shape[-1]))
    h = jnp.concatenate([meta, x], axis=1)
    lbf_all = jnp.cumsum(jax.nn.softmax(lb_fwd.astype(jnp.float32), axis=0), axis=0)
    lbb_all = jnp.cumsum(jax.nn.softmax(lb_bwd.astype(jnp.float32), axis=0), axis=0)
    for l in range(DEPTH_2):
        a = rms_norm(h, norm_mix[l])
        p = a @ w_in[l]
        y_hy = hyena_mixer(p[..., :D_HYENA_PROJ], conv_w[l], conv_b[l], filt_w1[l], filt_b1[l],
                           filt_w2[l], filt_b2[l], filt_w3[l], filt_freq[l], filt_skip[l])
        y_hy = rms_norm(y_hy, hyena_norm[l])
        y_hg = hgrn2_mixer(p[..., D_HYENA_PROJ:], lbf_all[l], lbb_all[l], hgrn_norm[l])
        h = h + jnp.concatenate([y_hy, y_hg], axis=-1) @ w_out[l]
        h = h + hier_moe(rms_norm(h, norm_ffn[l]), w_router_group[l], w_router_expert[l],
                         w_gate[l], w_up[l], w_down[l])
    h = rms_norm(h, norm_final)
    return h[:, N_META:]


def setup_inputs(seed=0):
    out = dict(first_inputs(seed))
    for name, value in second_inputs(seed + 1).items():
        if name != "x":
            out[name + "_2"] = value
    return out


def reference(
    x, c, cond_w, cond_b, ada_w, ada_b, ln_g, ln_b, ffn_up, ffn_conv_w, ffn_conv_b, ffn_down,
    gdn_w_in, gdn_conv_w, gdn_a_log, gdn_dt_bias, gdn_norm_w, gdn_w_out, ret_w_in, ret_w_out,
    gmlp_w_in, gmlp_ln_g, gmlp_ln_b, gmlp_w_s, gmlp_b_s, gmlp_w_out, sb_w_in, sb_w_out,
    meta_tokens_2, w_in_2, conv_w_2, conv_b_2, filt_w1_2, filt_b1_2, filt_w2_2, filt_b2_2,
    filt_w3_2, filt_freq_2, filt_skip_2, hyena_norm_2, lb_fwd_2, lb_bwd_2, hgrn_norm_2, w_out_2,
    norm_mix_2, norm_ffn_2, w_router_group_2, w_router_expert_2, w_gate_2, w_up_2, w_down_2,
    norm_final_2,
):
    x = first_block(
        x, c, cond_w, cond_b, ada_w, ada_b, ln_g, ln_b, ffn_up, ffn_conv_w, ffn_conv_b,
        ffn_down, gdn_w_in, gdn_conv_w, gdn_a_log, gdn_dt_bias, gdn_norm_w, gdn_w_out, ret_w_in,
        ret_w_out, gmlp_w_in, gmlp_ln_g, gmlp_ln_b, gmlp_w_s, gmlp_b_s, gmlp_w_out, sb_w_in,
        sb_w_out,
    )
    return second_block(
        x, meta_tokens_2, w_in_2, conv_w_2, conv_b_2, filt_w1_2, filt_b1_2, filt_w2_2,
        filt_b2_2, filt_w3_2, filt_freq_2, filt_skip_2, hyena_norm_2, lb_fwd_2, lb_bwd_2,
        hgrn_norm_2, w_out_2, norm_mix_2, norm_ffn_2, w_router_group_2, w_router_expert_2,
        w_gate_2, w_up_2, w_down_2, norm_final_2,
    )


_drawn_inputs = setup_inputs


def setup_inputs(seed=0):
    import zlib

    import numpy as np

    out = dict(_drawn_inputs(seed))
    spreads = {}
    factors = {'cond_b': 8.0,
     'ffn_conv_b': 5.283,
     'gdn_norm_w': 4.661,
     'filt_freq_2': 5.782,
     'hyena_norm_2': 4.519,
     'lb_fwd_2': 7.282,
     'lb_bwd_2': 8.0,
     'hgrn_norm_2': 6.347,
     'norm_mix_2': 2.973,
     'norm_ffn_2': 3.788,
     'norm_final_2': 5.65}
    for name, (base, spread) in spreads.items():
        noise = np.random.default_rng([zlib.crc32(name.encode()), seed]).standard_normal(out[name].shape)
        drawn = base * np.exp(spread * noise) if base else spread * noise
        out[name] = __import__('jax').numpy.asarray(drawn.astype(out[name].dtype))
    for name, factor in factors.items():
        out[name] = (out[name] * factor).astype(out[name].dtype)
    return out
```

```python
from contextlib import ExitStack

import numpy as np

import concourse.bass as bass
from concourse import mybir

ALU = mybir.AluOpType
ACT = mybir.ActivationFunctionType
AX = mybir.AxisListType
F32 = mybir.dt.float32
FR = mybir.dt.float32r
U32 = mybir.dt.uint32
I32 = mybir.dt.int32

P = 128
D = 1024
KD = D // P
T = 512
TT = T // P
DEPTH = 2
ALPHA = (2.0 * DEPTH) ** 0.25
LN_EPS = 1e-5
EPS = 1e-6

GH = 8
GDN_CONV = 4
GC = P
GCN = T // GC
LEVELS = GC.bit_length() - 1

RH = 4
R_DK = D // RH
R_DV = 2 * D // RH
R_VT = R_DV // P

F = 2816
FT = F // P
FFN_CONV = 3

N_META = 16
L2 = T + N_META
HALF = L2 // 2
W_HY = 512
HYT = W_HY // P
N_FREQ = L2 + 1
FQT = -(-N_FREQ // P)
CH = 64
NCH = T // CH

N_GROUPS = 8
PER_GROUP = 8
NE = N_GROUPS * PER_GROUP
D_EXP = D // 2
SLOTS = 64
CHOICES = 2 * T
OVER = (CHOICES - 1) // SLOTS
N_SLOTS = (NE + OVER) * SLOTS

SLOT_W = FT * P
NSLOT = 4

PARAM_TABLES = [
    [("gdn_conv_w", GDN_CONV * 3 * GH), ("gdn_norm_w", 1), ("cond_b", KD), ("c", KD)],
    [("ada_b", DEPTH * 6 * KD), ("ln_g", DEPTH * 2 * KD)],
    [("ln_b", DEPTH * 2 * KD), ("ffn_conv_b", DEPTH * FT), ("conv_w_2", 3 * 3 * HYT), ("conv_b_2", 3 * HYT)],
    [("filt_skip_2", 2 * HYT), ("hyena_norm_2", HYT), ("hgrn_norm_2", HYT), ("lb_fwd_2", 2 * HYT),
     ("lb_bwd_2", 2 * HYT), ("norm_mix_2", KD), ("norm_ffn_2", KD)],
    [("ffn_conv_w", DEPTH * FFN_CONV * FT)],
]


def shape_tables():
    i = np.arange(P)
    out = {}
    out["t_ident"] = np.eye(P)
    out["t_upper"] = (i[:, None] <= i[None, :]) * 1.0
    out["t_strict"] = (i[:, None] < i[None, :]) * 1.0
    out["t_levels"] = np.stack([
        ((i[:, None] // (2 * s) == i[None, :] // (2 * s)) & (i[:, None] % (2 * s) < s) & (i[None, :] % (2 * s) >= s)) * 1.0
        for s in (1, 2, 4, 8, 16, 32, 64)], 1)
    inv = (np.float32(10000.0) ** (-np.linspace(0.0, 1.0, R_DK // 2, dtype=np.float32))).astype(np.float32)
    ang = (np.arange(T, dtype=np.float32)[None, :] * inv[:, None]).astype(np.float64)
    out["t_rope"] = np.stack([np.cos(ang), np.sin(ang)], 1)
    rel = np.arange(T)[None, :] - i[:, None]
    out["t_decay"] = np.stack([
        np.where(rel >= 0, (1.0 - 2.0 ** (-5.0 - h)) ** np.maximum(rel, 0), 0.0) * R_DK ** -0.5 for h in range(RH)], 1)
    n = np.arange(FQT * P)
    ph = (n[:, None] * n[None, :N_FREQ]) % (2 * L2) * (np.pi / L2)
    live = (n[:, None] < N_FREQ) * 1.0
    out["t_cos"] = (np.cos(ph) * live).reshape(FQT, P, N_FREQ).transpose(1, 0, 2)
    out["t_sin"] = (np.sin(ph) * live).reshape(FQT, P, N_FREQ).transpose(1, 0, 2)
    wk = np.where((n == 0) | (n == L2), 1.0, 2.0) / (2 * L2)
    out["t_wk"] = wk.reshape(FQT, P).T
    t = (np.arange(L2, dtype=np.float32) / np.float32(L2 - 1)).astype(np.float32)
    bands = np.linspace(1e-4, 15, 16, dtype=np.float32)
    a2 = (np.float32(2.0 * np.pi / L2) * np.arange(L2, dtype=np.float32)[:, None] * bands[None, :]).astype(np.float64)
    out["t_emb"] = np.concatenate([t[:, None], np.cos(a2), -np.sin(a2)], -1).T
    deltas = np.abs(np.linspace(np.log(1e-2) / 1.5, np.log(1e-2) / 0.3, W_HY, dtype=np.float32))
    win = np.zeros((FQT * P, W_HY))
    win[:L2] = np.exp((-t[:, None] * deltas[None, :]).astype(np.float64))
    out["t_window"] = win.reshape(FQT, P, W_HY).transpose(1, 0, 2)
    out["t_not_first"] = (i[:, None] > 0) * 1.0
    starts, ends = np.ones(L2), np.ones(L2)
    starts[[0] + [N_META + CH * c for c in range(NCH)]] = 0.0
    ends[[N_META - 1] + [N_META + CH * c + CH - 1 for c in range(NCH)]] = 0.0
    out["t_runs"] = np.broadcast_to(np.stack([starts, ends[::-1]])[None], (P, 2, L2))
    out["t_countdown"] = np.broadcast_to(8.0 - np.arange(8)[None, :], (P, 8))
    out["t_expert"] = np.broadcast_to(np.arange(NE)[None, :] * 1.0, (P, NE))
    return {k: np.ascontiguousarray(v, dtype=np.float32) for k, v in out.items()}


class Steps:

    def __init__(self, eng, sem):
        self.eng, self.sem, self.n, self.shift = eng, sem, 0, 0

    def done(self, ins):
        ins.then_inc(self.sem, 1)
        self.n += 1
        return self.n

    def wait(self, n=None):
        self.eng.wait_ge(self.sem, self.shift + (self.n if n is None else n))

    def enter(self, i, per):
        self.start, self.per, self.shift = self.n, per, i * per

    def leave(self, times):
        assert self.n - self.start == self.per, (self.n - self.start, self.per)
        self.n, self.shift = self.start + self.per * times, 0


class Signals:

    def __init__(self, k, kind, **totals):
        self.k, self.kind = k, kind
        self.past = {what: k.signalled.get((kind, what), 0) for what in totals}
        for what, n in totals.items():
            k.signalled[kind, what] = self.past[what] + n

    def sem(self, what):
        return self.k.sem(f"{self.kind}_{what}")

    def wait(self, eng, what, n):
        eng.wait_ge(self.sem(what), n + self.past.get(what, 0))


class Core:

    def __init__(self, nc, ctx, ins, tables, out, x_slots, y_slots):
        self.nc, self.ctx, self.ins, self.tables, self.out = nc, ctx, ins, tables, out
        self.x_slots, self.y_slots = x_slots, y_slots
        self.sems = {}
        self.signalled = {}
        self.tables_issued, self.tables_due = 0, {}
        self.at = {}

        def sb(name, shape, dtype=F32):
            self.at[name] = -(-nc.sbuf_base // 32) * 32
            return ctx.enter_context(nc.sbuf_tensor(name, shape, dtype))

        self.sb = sb
        self.xT = self.sb("xT", [P, KD, T])
        self.hT = self.sb("hT", [P, KD, L2])
        self.ring = self.sb("ring", [P, NSLOT, SLOT_W])
        self.ident = self.sb("ident", [P, P])
        self.ones = self.sb("ones", [P, P])
        self.mean = self.sb("mean", [P, P])
        self.eps = self.sb("eps", [P, 2])
        self.par = self.sb("par", [P, len(PARAM_TABLES) + 1, P])
        self.mod = self.sb("mod", [P, DEPTH, 6, KD])
        self.e = self.sb("e", [P, KD])
        self.spare = self.sb("spare", [P, D])
        self.arena = self.sb("arena", [P, ARENA_W])
        self.views = {}
        self.ps = ctx.enter_context(nc.psum_tensor("ps", [P, 8, 512], F32))
        self.param_at = {}
        for n, table in enumerate(PARAM_TABLES):
            at = n * P
            for name, rows in table:
                self.param_at[name] = at
                at += rows
        self.meets = {}
        self.base = 14

    def sem(self, name):
        if name not in self.sems:
            self.sems[name] = self.ctx.enter_context(self.nc.semaphore(name))
        return self.sems[name]

    def as_parts(self, ap):
        n, name = int(np.prod(ap.shape[1:])), ap.tensor.name
        if (name, ap.offset, n) not in self.views:
            self.views[name, ap.offset, n] = self.nc.alloc_sbuf_tensor_at(f"{name}_parts_{ap.offset}_{n}", [P, n], FR, offset=self.at[name] + 4 * ap.offset)
        flat = self.views[name, ap.offset, n][:]
        return flat if len(ap.shape) == 2 else flat.rearrange("p (k c) -> p k c", k=ap.shape[1])

    def col(self, name, j):
        flat = self.par[:].rearrange("p t c -> p (t c)")
        at = self.param_at[name]
        return flat[:, at + j:at + j + 1] if isinstance(j, int) else flat[:, bass.ds(j + at, 1)]

    def cols(self, name, j, n):
        flat = self.par[:].rearrange("p t c -> p (t c)")
        at = self.param_at[name]
        return flat[:, at + j:at + j + n]

    def load_tables(self, sp, name, pairs):
        for to, source in pairs:
            sp.dma_start(to, source).then_inc(self.sem("tables_in"), 16)
            self.tables_issued += 16
        self.tables_due[name] = self.tables_issued

    def wait_tables(self, eng, name):
        eng.wait_ge(self.sem("tables_in"), self.tables_due[name])

    def meet(self, eng, who):
        eng.drain().then_inc(self.sem("stage_ended"), 1)
        self.meets[who] = self.meets.get(who, 0) + 1
        eng.wait_ge(self.sem("stage_ended"), 4 * self.meets[who])

    def stage_over(self, eng, n):
        eng.wait_ge(self.sem("stage_ended"), 4 * n)


ARENA_W = 30720


class Room:

    def __init__(self, *regions):
        self.regions = [[r, 0] for r in regions]

    def take(self, *shape):
        n = int(np.prod(shape))
        for r in self.regions:
            if r[1] + n <= r[0].shape[1]:
                at = r[1]
                r[1] += n
                flat = r[0][:, at:at + n]
                if len(shape) == 1:
                    return flat
                names = "abcd"[:len(shape)]
                return flat.rearrange(f"p ({' '.join(names)}) -> p {' '.join(names)}", **dict(zip(names, shape)))
        raise MemoryError(f"{shape}: {[(r[0].shape, r[1]) for r in self.regions]}")



def tiles_of(w):
    return w.rearrange("(k p) n -> p k n", p=P)


class Stream:

    def __init__(self, core):
        self.core, self.n, self.groups, self.splits = core, 0, 0, 0

    def slot(self, n, kt, cols):
        flat = self.core.ring[:, n % NSLOT, 0:kt * cols]
        return flat.rearrange("p (k c) -> p k c", k=kt)

    def load(self, sp, n, i, source, kt, cols):
        c = self.core
        if n >= NSLOT or not isinstance(i, int):
            sp.wait_ge(c.sem("chunk_used"), i * NSLOT + (n - NSLOT + 1))
        sp.dma_start(self.slot(n, kt, cols), source).then_inc(c.sem(f"chunk_in_slot{n % NSLOT}"), 16)

    def landed(self, pe, n, i):
        pe.wait_ge(self.core.sem(f"chunk_in_slot{n % NSLOT}"), i * 16 + 16 * (n // NSLOT + 1))

    def group_done(self, ins, last):
        ins.then_inc(self.core.sem("chunk_used" if last else "group_summed"), 1)

    def wait_group(self, eng, n, i, c, f):
        if f == self.per - 1:
            eng.wait_ge(self.core.sem("chunk_used"), i * NSLOT + (n + 1))
        else:
            eng.wait_ge(self.core.sem("group_summed"), i * (NSLOT * (self.per - 1)) + (self.groups + (self.per - 1) * c + f + 1))


    def upper(self, room, n, kt, cols):
        return self.core.as_parts(room[:, n % 2, 0:kt * cols].rearrange("p (k c) -> p k c", k=kt))

    def lower(self, n, kt, cols):
        return self.core.as_parts(self.slot(n, kt, cols))

    def round_chunk(self, act, room, n, i, kt, cols, wait=True):
        self.landed(act, n, i)
        if wait:
            act.wait_ge(self.core.sem("chunk_used"), i * NSLOT + (n - 1))
        act.activation(self.upper(room, n, kt, cols), self.slot(n, kt, cols), ACT.Copy).then_inc(self.core.sem("chunk_rounded"), 1)

    def lower_chunks(self, pool, room, chunks, per, kt, cols):
        def chunk(n, i, c):
            pool.wait_ge(self.core.sem("chunk_rounded"), i * NSLOT + (self.splits + c + 1))
            pool.tensor_tensor(self.lower(n, kt, cols), self.slot(n, kt, cols), self.upper(room, n, kt, cols), ALU.subtract)\
                .then_inc(self.core.sem("chunk_split"), 1)
        self.rounds(pool, chunks, per, chunk, True)

    def split_landed(self, pe, n, i, c):
        pe.wait_ge(self.core.sem("chunk_split"), i * NSLOT + (self.splits + c + 1))

    def load_run(self, sp, sources, kt, cols, chunks, beside=None):
        k = len(sources)
        def one(n, i, c):
            src = sources[c % k]
            at = c // k * cols if isinstance(i, int) else i * (NSLOT // k * cols) + c // k * cols
            self.load(sp, self.n + n, i, src[:, :, bass.ds(at, cols)], kt, cols)
        first = 0
        if self.n < NSLOT:
            for c in range(NSLOT):
                one(c, 0, c)
            first = 1
        rounds = chunks // NSLOT
        if rounds - first > 1:
            with sp.Fori(first, rounds) as i:
                for s in range(NSLOT):
                    one(s, i, s)
                    if beside:
                        beside(i, s)
            first = rounds
        for c in range(first * NSLOT, chunks):
            one(c, 0, c)
            if beside:
                beside(0, c)
        self.n += chunks

    def rounds(self, eng, chunks, per, body, splits=False):
        self.per = per
        rounds = chunks // NSLOT
        if rounds > 1:
            with eng.Fori(0, rounds) as i:
                for s in range(NSLOT):
                    body(self.n + s, i, s)
        elif rounds == 1:
            for s in range(NSLOT):
                body(self.n + s, 0, s)
        for c in range(rounds * NSLOT, chunks):
            body(self.n + c, 0, c)
        self.skip(chunks, per, splits)

    def skip(self, chunks, per, splits=False):
        self.n += chunks
        self.groups += (per - 1) * chunks
        self.splits += chunks if splits else 0


class SplitInput(Signals):

    def __init__(self, k, tiles, source, room, width=T):
        super().__init__(k, "input", rounded=tiles, split=tiles)
        self.tiles, self.source = tiles, source
        rounded = room.take(tiles, width)
        self.upper = [k.as_parts(rounded[:, r, :]) for r in range(tiles)]
        self.lower = [k.as_parts(source(r)) for r in range(tiles)]

    def scalar(self, act):
        for r in range(self.tiles):
            act.activation(self.upper[r], self.source(r), ACT.Copy).then_inc(self.sem("rounded"), 1)

    def vector(self, dve):
        for r in range(self.tiles):
            self.wait(dve, "rounded", r + 1)
            dve.tensor_tensor(self.lower[r], self.source(r), self.upper[r], ALU.subtract).then_inc(self.sem("split"), 1)

    def products(self, pe, out, upper, lower, first, part=slice(None)):
        for r in range(self.tiles):
            if first:
                self.wait(pe, "split", r + 1)
            pe.matmul(out, upper[:, r], self.upper[r][:, part], start=(r == 0), stop=False)
            pe.matmul(out, upper[:, r], self.lower[r][:, part], start=False, stop=False)
            ins = pe.matmul(out, lower[:, r], self.upper[r][:, part], start=False, stop=(r == self.tiles - 1))
        return ins



class Setup:
    def __init__(self, k):
        self.k = k
        room = Room(k.arena)
        self.rows = room.take(len(PARAM_TABLES) + 1, P)
        self.x_in = room.take(TT, D)

    def sync(self, sp):
        k = self.k
        sp.dma_start(k.ident[:], k.tables["t_ident"]).then_inc(k.sem("ident_in"), 16)
        n = 0
        for t, table in enumerate(PARAM_TABLES):
            at = 0
            for name, rows in table:
                for r0 in range(0, rows, P):
                    r = min(P, rows - r0)
                    src = k.ins[name].rearrange("(r c) -> r c", c=P)[r0:r0 + r]
                    where = t if r0 == 0 else len(PARAM_TABLES)
                    sp.dma_start(self.rows[at:at + r, where, :] if r0 == 0 else self.rows[0:r, where, :], src).then_inc(k.sem("params_in"), 16)
                    n += 1
                at += rows
        self.param_loads = n
        sp.dma_start(self.x_in, k.ins["x"].rearrange("(t p) d -> p t d", p=P)).then_inc(k.sem("x_in"), 16)

    def table_rows(self):
        for t, table in enumerate(PARAM_TABLES):
            total = sum(r for _, r in table)
            yield t, min(total, P), t * P
            if total > P:
                assert len(table) == 1
                yield len(PARAM_TABLES), total - P, t * P + P

    def gpsimd(self, pool):
        k = self.k
        pool.memset(k.ones[:], 1.0)
        pool.memset(k.mean[:], 1.0 / D)
        pool.memset(k.eps[:, 0:1], LN_EPS)
        pool.memset(k.eps[:, 1:2], EPS)

    def tensor(self, pe):
        k = self.k
        pe.wait_ge(k.sem("ident_in"), 16)
        pe.wait_ge(k.sem("params_in"), 16 * self.param_loads)
        for n, (t, rows, _) in enumerate(self.table_rows()):
            pe.transpose(k.ps[:, n, 0:rows], self.rows[0:rows, t, :], k.ident[0:rows, 0:rows]).then_inc(k.sem("table_turned"), 1)
        pe.wait_ge(k.sem("x_in"), 16)
        for j in range(KD):
            bank = 6 + j % 2
            if j >= 2:
                pe.wait_ge(k.sem("x_copied"), j - 1)
            for t in range(TT):
                ins = pe.transpose(k.ps[:, bank, t * P:(t + 1) * P], self.x_in[:, t, j * P:(j + 1) * P], k.ident[:])
            ins.then_inc(k.sem("x_turned"), 1)

    def vector(self, dve):
        k = self.k
        flat = k.par[:].rearrange("p t c -> p (t c)")
        for n, (_, rows, at) in enumerate(self.table_rows()):
            dve.wait_ge(k.sem("table_turned"), n + 1)
            dve.tensor_copy(flat[:, at:at + rows], k.ps[:, n, 0:rows])
        for j in range(KD):
            dve.wait_ge(k.sem("x_turned"), j + 1)
            dve.tensor_copy(k.xT[:, j, :], k.ps[:, 6 + j % 2, :]).then_inc(k.sem("x_copied"), 1)

    def scalar(self, act):
        pass



class Conditioning:

    W = D
    PER_LAYER = 6

    def __init__(self, k):
        self.k = k
        room = Room(k.arena)
        self.w = room.take(2, KD, self.W)
        self.acc = room.take(2, self.W)
        self.e = k.e[:]
        self.e_pre = room.take(KD)

    def chunks(self, eng, body):
        body(0, 0, None, 0)
        for l in range(1):
            with eng.Fori(0, self.PER_LAYER // 2) as i:
                for s in range(2):
                    body(1 + self.PER_LAYER * l + s, i, l, s)

    def sync(self, sp):
        k = self.k

        def load(n, i, l, m):
            sp.wait_ge(k.sem("cond_w_free"), i * 2 + (n + 1))
            src = tiles_of(k.ins["cond_w"]) if l is None else \
                tiles_of(k.ins["ada_w"][l])[:, :, bass.ds(i * (2 * self.W) + m * self.W, self.W)]
            sp.dma_start(self.w[:, n % 2], src).then_inc(k.sem(f"cond_w_in{n % 2}"), 16)

        self.chunks(sp, load)

    def vector(self, dve, st):
        k = self.k
        dve.sem_inc(k.sem("cond_w_free"), 2)

        def chunk(n, i, l, m):
            dve.wait_ge(k.sem(f"cond_w_in{n % 2}"), i * 16 + 16 * (n // 2 + 1))
            dve.wait_ge(k.sem("cond_acc_free"), i * 2 + (n + 1))
            acc = self.acc[:, n % 2]
            if l is not None:
                st.enter(i, 2 * (KD - 1)) if m == 0 else None
            for r in range(KD):
                v = k.col("c", r) if l is None else self.e[:, r:r + 1]
                w = self.w[:, n % 2, r, :]
                if r == 0:
                    ins = dve.tensor_scalar(acc, w, v, None, ALU.mult)
                else:
                    st.wait()
                    ins = dve.scalar_tensor_tensor(acc, w, v, acc, ALU.mult, ALU.add)
                if r < KD - 1:
                    st.done(ins)
            ins.then_inc(k.sem("cond_w_free"), 1)
            if l is None:
                dve.wait_ge(k.sem("cond_acc_free"), 3)
                dve.tensor_tensor(self.e_pre, k.ps[:, 2, 0:KD], k.cols("cond_b", 0, KD), ALU.add).then_inc(k.sem("e_biased"), 1)
                dve.wait_ge(k.sem("e_ready"), 1)
            elif m == 1:
                st.leave(self.PER_LAYER // 2)

        self.chunks(dve, chunk)
        for l in range(1):
            dve.wait_ge(k.sem("cond_acc_free"), 2 + 1 + self.PER_LAYER * (l + 1))
            mod = k.mod[:, l].rearrange("p m j -> p (m j)")
            st.done(dve.tensor_tensor(mod, k.ps[:, l, 0:6 * KD], k.cols("ada_b", l * 6 * KD, 6 * KD), ALU.add))
            st.wait()
            for a in (1, 4):
                two = k.mod[:, l, a:a + 2, :]
                dve.tensor_scalar(two, two, 1.0, None, ALU.add).then_inc(k.sem("mod_ready"), 1)
        for j in range(KD):
            dve.wait_ge(k.sem("h_ready"), j + 1)
            dve.tensor_scalar(k.xT[:, j, :], k.xT[:, j, :], ALPHA, None, ALU.mult)

    def tensor(self, pe):
        k = self.k
        pe.sem_inc(k.sem("cond_acc_free"), 2)

        def sums(n, i, l, m):
            pe.wait_ge(k.sem("cond_w_free"), i * 2 + (n + 3))
            for f in range(KD):
                out = k.ps[:, 2, f:f + 1] if l is None else k.ps[:, l, bass.ds(i * (2 * KD) + (m * KD + f), 1)]
                ins = pe.matmul(out, self.acc[:, n % 2, f * P:(f + 1) * P], k.ones[:, 0:1], start=True, stop=True)
            ins.then_inc(k.sem("cond_acc_free"), 1)

        self.chunks(pe, sums)

    def scalar(self, act):
        k = self.k
        act.wait_ge(k.sem("e_biased"), 1)
        act.activation(self.e, self.e_pre, ACT.Silu).then_inc(k.sem("e_ready"), 1)
        act.wait_ge(k.sem("mod_ready"), 2)
        for j in range(KD):
            act.activation(k.hT[:, j, 0:T], k.xT[:, j, :], ACT.Identity, bias=k.mod[:, 0, 0, j:j + 1],
                           scale=k.mod[:, 0, 1, j:j + 1]).then_inc(k.sem("h_ready"), 1)

    def gpsimd(self, pool):
        pass


class NextConditioning:

    W = D // 2
    COUNT = 6 * D // W
    PAST = 2 + 1 + Conditioning.PER_LAYER
    BANK = 4

    def __init__(self, k, room):
        self.k = k
        self.w = room.take(2, KD, self.W)
        self.acc = room.take(2, self.W)

    def sync(self, sp, i, u):
        k = self.k
        k.stage_over(sp, 7)
        sp.wait_ge(k.sem("cond_w_free"), i * 2 + (u + self.PAST - 1))
        src = tiles_of(k.ins["ada_w"][1])[:, :, bass.ds(i * (2 * self.W) + u * self.W, self.W)]
        sp.dma_start(self.w[:, u], src).then_inc(k.sem(f"cond_w_in{u}"), 16)

    def vector(self, dve, st, i, u):
        k, acc = self.k, self.acc[:, u]
        dve.wait_ge(k.sem(f"cond_w_in{u}"), i * 16 + 16 * (4 - u + 1))
        dve.wait_ge(k.sem("cond_acc_free"), i * 2 + (u + self.PAST - 1))
        for r in range(KD):
            if r == 0:
                ins = dve.tensor_scalar(acc, self.w[:, u, r, :], k.e[:, r:r + 1], None, ALU.mult)
            else:
                st.wait()
                ins = dve.scalar_tensor_tensor(acc, self.w[:, u, r, :], k.e[:, r:r + 1], acc, ALU.mult, ALU.add)
            if r < KD - 1:
                st.done(ins)
        ins.then_inc(k.sem("cond_w_free"), 1)

    def tensor(self, pe, i, u):
        k = self.k
        pe.wait_ge(k.sem("cond_w_free"), i * 2 + (u + self.PAST + 1))
        per = self.W // P
        for f in range(per):
            ins = pe.matmul(k.ps[:, self.BANK, bass.ds(i * (2 * per) + (u * per + f), 1)], self.acc[:, u, f * P:(f + 1) * P], k.ones[:, 0:1], start=True, stop=True)
        ins.then_inc(k.sem("cond_acc_free"), 1)

    def finish(self, dve, st):
        k = self.k
        dve.wait_ge(k.sem("cond_acc_free"), self.PAST + self.COUNT)
        mod = k.mod[:, 1].rearrange("p m j -> p (m j)")
        st.done(dve.tensor_tensor(mod, k.ps[:, self.BANK, 0:6 * KD], k.cols("ada_b", 6 * KD, 6 * KD), ALU.add))
        st.wait()
        for a in (1, 4):
            two = k.mod[:, 1, a:a + 2, :]
            dve.tensor_scalar(two, two, 1.0, None, ALU.add)



class DeltaIn:

    BANKS = 4

    def __init__(self, k, stream):
        self.k, self.stream = k, stream
        room = Room(k.arena)
        self.tiles = room.take(4 * GH, T)
        self.rest = k.arena[:, 4 * GH * T:]
        room = Room(self.rest)
        self.kept = room.take(2, T)
        self.g_rows = self.kept[0:GH, 0, :]
        self.b_rows = self.kept[0:GH, 1, :]
        self.colm = room.take(3, GCN, GH)
        self.upper = room.take(P)
        self.strict = room.take(P)
        self.levels = k.spare[:, 0:LEVELS * P].rearrange("p (l c) -> p l c", c=P)
        self.free_at = room.regions[0][1]
        self.pre = room.take(self.BANKS, T)
        self.w_upper = room.take(2, KD * 2 * P)
        self.input = SplitInput(k, KD, lambda r: k.hT[:, r, 0:T], room)
        self.w_gate = room.take(KD, 2 * GH)
        self.head = room.take(2, 1)
        self.rows = room.take(4, T)

    def sync(self, sp):
        k = self.k
        w = tiles_of(k.ins["gdn_w_in"])
        k.stage_over(sp, 2)
        row = lambda name: k.ins[name].rearrange("(h o) -> h o", o=1)
        k.load_tables(sp, "gdn", [
            (self.w_gate, w[:, :, 4 * GH * P:4 * GH * P + 2 * GH]),
            (self.head[0:GH, 0, :], row("gdn_a_log")), (self.head[0:GH, 1, :], row("gdn_dt_bias")),
            (self.upper, k.tables["t_upper"]), (self.strict, k.tables["t_strict"]), (self.levels, k.tables["t_levels"])])
        self.stream.load_run(sp, [w], KD, 2 * P, 2 * GH)

    def tensor(self, pe, stream):
        k = self.k
        pe.wait_ge(k.sem("h_ready"), KD)
        k.wait_tables(pe, "gdn")
        for half in range(2):
            for r in range(KD):
                ins = pe.matmul(k.ps[0:GH, 4 + half, :], self.w_gate[:, r, half * GH:(half + 1) * GH], k.hT[:, r, 0:T],
                                start=(r == 0), stop=(r == KD - 1))
            ins.then_inc(k.sem("gate_logits"), 1)
        pe.sem_inc(k.sem("gdn_convolved"), self.BANKS)
        pe.sem_inc(k.sem("gdn_z_ready"), self.BANKS)

        def products(freed, first):
            def chunk(n, i, c):
                stream.split_landed(pe, n, i, c)
                lower, upper = stream.lower(n, KD, 2 * P), stream.upper(self.w_upper, n, KD, 2 * P)
                for f in range(2):
                    g = 2 * c + f
                    pe.wait_ge(k.sem(freed), i * (2 * NSLOT) + (g + 1))
                    at = slice(f * P, (f + 1) * P)
                    ins = self.input.products(pe, k.ps[:, g % self.BANKS, :], upper[:, :, at], lower[:, :, at], first and g == 0)
                    stream.group_done(ins, f == 1)
            return chunk

        stream.rounds(pe, 3 * GH // 2, 2, products("gdn_convolved", True), True)
        pe.wait_ge(k.sem("gdn_convolved"), self.BANKS + 3 * GH)
        stream.rounds(pe, GH // 2, 2, products("gdn_z_ready", False), True)
        pe.wait_ge(k.sem("gate_rows"), 5)
        for what, rows in enumerate((self.g_rows, self.b_rows)):
            for t in range(GCN):
                at = (what * GCN + t) * GH
                ins = pe.transpose(k.ps[:, 6, at:at + GH], rows[:, t * P:(t + 1) * P], k.ident[0:GH, 0:GH])
        ins.then_inc(k.sem("gate_cols"), 1)

    def vector(self, dve, st, stream):
        k = self.k
        dve.sem_inc(k.sem("gdn_silu"), self.BANKS)
        x, e, g = self.rows[0:GH, 0, :], self.rows[0:GH, 1, :], self.rows[0:GH, 2, :]
        one = self.rows[0:GH, 3, :]
        st.done(dve.memset(one, 1.0))
        dve.wait_ge(k.sem("gate_logits"), 2)
        dve.tensor_scalar(x, k.ps[0:GH, 4, :], self.head[0:GH, 1, :], None, ALU.add).then_inc(k.sem("gate_x"), 1)
        self.input.vector(dve)
        dve.wait_ge(k.sem("gate_exp"), 2)
        dve.tensor_scalar(e, e, 1.0, None, ALU.add).then_inc(k.sem("gate_x"), 1)
        dve.wait_ge(k.sem("gate_exp"), 4)
        st.done(dve.scalar_tensor_tensor(g, x, 0.0, e, ALU.max, ALU.add))
        st.wait()
        st.done(dve.tensor_scalar(g, g, self.head[0:GH, 0, :], -1.0, ALU.mult, ALU.mult))
        st.wait()
        for t in range(GCN):
            at = slice(t * P, (t + 1) * P)
            dve.tensor_tensor_scan(self.g_rows[:, at], one[:, at], g[:, at], 0.0, ALU.mult, ALU.add).then_inc(k.sem("gate_rows"), 1)

        def conv(n, i, c):
            if c == 0:
                st.enter(i, 2 * NSLOT * (GDN_CONV - 1))
            for f in range(2):
                tile = 2 * c + f
                stream.wait_group(dve, n, i, c, f)
                pre, src = self.pre[:, tile % self.BANKS], k.ps[:, tile % self.BANKS]
                dve.wait_ge(k.sem("gdn_silu"), i * (2 * NSLOT) + (tile + 1))
                for back in range(GDN_CONV):
                    w = k.col("gdn_conv_w", i * (2 * NSLOT) + ((GDN_CONV - 1 - back) * 3 * GH + tile))
                    if back == 0:
                        st.done(dve.tensor_scalar(pre, src, w, None, ALU.mult))
                        continue
                    st.wait()
                    ins = dve.scalar_tensor_tensor(pre[:, back:], src[:, 0:T - back], w, pre[:, back:], ALU.mult, ALU.add)
                    if back < GDN_CONV - 1:
                        st.done(ins)
                ins.then_inc(k.sem("gdn_convolved"), 1)
            if c == NSLOT - 1:
                st.leave(3 * GH // 2 // NSLOT)

        stream.rounds(dve, 3 * GH // 2, 2, conv, True)
        stream.skip(GH // 2, 2, True)
        dve.wait_ge(k.sem("gate_cols"), 1)
        cols = self.colm.rearrange("p w t h -> p (w t h)")
        two = 2 * GCN * GH
        dve.tensor_copy(cols[:, 0:two], k.ps[:, 6, 0:two]).then_inc(k.sem("gate_cols_copied"), 1)
        dve.wait_ge(k.sem("gate_exp"), 5)
        st.done(dve.scalar_tensor_tensor(self.colm[:, 2], self.colm[:, 2], -1.0, self.colm[:, 1], ALU.mult, ALU.mult))

    def scalar(self, act, stream):
        k = self.k
        round_chunk = lambda n, i: stream.round_chunk(act, self.w_upper, n, i, KD, 2 * P, False)
        round_chunk(0, 0)
        self.input.scalar(act)
        act.wait_ge(k.sem("gate_logits"), 2)
        act.activation(self.b_rows, k.ps[0:GH, 5, :], ACT.Sigmoid).then_inc(k.sem("gate_rows"), 1)
        act.wait_ge(k.sem("gate_x"), 1)
        act.activation(self.rows[0:GH, 1, :], self.rows[0:GH, 0, :], ACT.Abs).then_inc(k.sem("gate_exp"), 1)
        act.wait_ge(k.sem("gate_exp"), 1)
        act.activation(self.rows[0:GH, 1, :], self.rows[0:GH, 1, :], ACT.Exp, scale=-1.0).then_inc(k.sem("gate_exp"), 1)
        k.wait_tables(act, "gdn")
        act.activation(self.head[0:GH, 0, :], self.head[0:GH, 0, :], ACT.Exp).then_inc(k.sem("gate_exp"), 1)
        act.wait_ge(k.sem("gate_x"), 2)
        act.activation(self.rows[0:GH, 1, :], self.rows[0:GH, 1, :], ACT.Ln).then_inc(k.sem("gate_exp"), 1)

        def silu(n, i, c):
            round_chunk(n + 1, i)
            for f in range(2):
                tile = 2 * c + f
                act.wait_ge(k.sem("gdn_convolved"), i * (2 * NSLOT) + (self.BANKS + tile + 1))
                act.activation(self.tiles[:, bass.ds(i * (2 * NSLOT) + tile, 1), :].rearrange("p o t -> p (o t)"), self.pre[:, tile % self.BANKS], ACT.Silu)\
                   .then_inc(k.sem("gdn_silu"), 1)

        def silu_z(n, i, c):
            if c + 1 < GH // 2:
                round_chunk(n + 1, i)
            for f in range(2):
                stream.wait_group(act, n, i, c, f)
                tile = 2 * c + f
                act.activation(self.tiles[:, 3 * GH + tile], k.ps[:, tile % self.BANKS], ACT.Silu).then_inc(k.sem("gdn_z_ready"), 1)

        stream.rounds(act, 3 * GH // 2, 2, silu, True)
        stream.rounds(act, GH // 2, 2, silu_z, True)
        act.wait_ge(k.sem("gate_cols_copied"), 1)
        act.activation(self.colm[:, 2], self.colm[:, 0], ACT.Exp).then_inc(k.sem("gate_exp"), 1)

    def gpsimd(self, pool, stream):
        stream.lower_chunks(pool, self.w_upper, 2 * GH, 2, KD, 2 * P)



class TileNorm(Signals):

    def __init__(self, k, room, pairs, source, scale, finish):
        super().__init__(k, "norm", squared=2 * pairs, summed=2 * pairs + 2, rooted=4 * pairs + 4, inverted=2 * pairs + 2)
        self.pairs, self.source = pairs, source
        self.scale, self.finish = scale, finish
        self.square = room.take(2, T)
        self.root = room.take(2, T)

    def scalar(self, act):
        k = self.k
        with act.Fori(0, self.pairs) as i:
            for u in range(2):
                self.wait(act, "summed", i * 2 + (u + 1))
                act.activation(self.square[:, u], self.source(i, u), ACT.Square).then_inc(self.sem("squared"), 1)
            for u in range(2):
                self.wait(act, "summed", i * 2 + (u + 3))
                self.wait(act, "inverted", i * 2 + (u + 1))
                act.activation(self.root[:, u], k.ps[:, u, :], ACT.Ln, bias=k.eps[:, 1:2], scale=self.scale).then_inc(self.sem("rooted"), 1)
            for u in range(2):
                self.wait(act, "rooted", i * 4 + (u + 5))
                act.activation(self.root[:, u], self.root[:, u], ACT.Exp, scale=-0.5).then_inc(self.sem("rooted"), 1)

    def tensor(self, pe):
        k = self.k
        pe.sem_inc(self.sem("summed"), 2)
        pe.sem_inc(self.sem("rooted"), 4)
        with pe.Fori(0, self.pairs) as i:
            for u in range(2):
                self.wait(pe, "squared", i * 2 + (u + 1))
                self.wait(pe, "rooted", i * 4 + (u + 1))
                pe.matmul(k.ps[:, u, :], k.ones[:], self.square[:, u], start=True, stop=True).then_inc(self.sem("summed"), 1)

    def vector(self, dve, st):
        dve.sem_inc(self.sem("inverted"), 2)
        with dve.Fori(0, self.pairs) as i:
            for u in range(2):
                self.wait(dve, "rooted", i * 4 + (u + 7))
                self.finish(dve, i, u, self.root[:, u], self)

    def gpsimd(self, pool):
        pass



def chunk_at(t):
    return slice(t * GC, (t + 1) * GC)


class DeltaHeads(Signals):

    LANES = 2

    def __init__(self, k, din):
        super().__init__(k, "heads", **{what: GH for what in ("turned", "masked", "diff", "exp", "o")})
        self.din = din
        room = Room(din.rest[:, din.free_at:], k.hT[:].rearrange("p j t -> p (j t)"))
        lanes = lambda *shape: [room.take(*shape) for _ in range(self.LANES)]
        self.kT, self.vT, self.vb, self.kb, self.kd = (lanes(T) for _ in range(5))
        self.decay, self.LT, self.qk, self.X, self.XT = (lanes(T) for _ in range(5))
        self.Ls, self.wT, self.qe, self.eg = (lanes(T) for _ in range(4))
        self.T1 = self.vT
        self.new = lanes(2, P)
        self.S = lanes(P)
        self.kdx = lanes(GCN)
        self.gm = [w[0:GH] for w in self.wT]
        self.bm = [x[0:GH] for x in self.X]
        self.iters = GH // self.LANES

    def count(self, i, lane, step=0, steps=1):
        return i * (self.LANES * steps) + (step * self.LANES + lane + 1)

    def bank(self, lane, b, t=None):
        ps = self.k.ps[:, 4 * lane + b, :]
        return ps if t is None else ps[:, chunk_at(t)]

    def tile(self, kind, i, lane):
        return self.din.tiles[:, bass.ds(i * self.LANES + (kind * GH + lane), 1), :].rearrange("p o t -> p (o t)")

    def lanes(self):
        return range(self.LANES)

    def gpsimd(self, pool):
        pool.sem_inc(self.sem("lane_free"), self.LANES)
        self.k.wait_tables(pool, "gdn")
        with pool.Fori(0, self.iters) as i:
            for lane in self.lanes():
                self.wait(pool, "lane_free", self.count(i, lane))
                for n, to in enumerate((self.kT, self.vT)):
                    pool.tensor_copy(to[lane], self.tile(1 + n, i, lane)).then_inc(self.sem("kv"), 1)
            for l in range(LEVELS):
                for lane in self.lanes():
                    if l == 0:
                        self.wait(pool, "lt", self.count(i, lane))
                    elif l == 1:
                        self.wait(pool, "x", self.count(i, lane, 0, LEVELS))
                    else:
                        self.wait(pool, "t1", self.count(i, lane, l - 1, LEVELS))
                    mask = self.din.levels[:, l, :].unsqueeze(1).to_broadcast([P, GCN, GC])
                    pool.tensor_tensor(self.Ls[lane].rearrange("p (t c) -> p t c", c=GC), self.LT[lane].rearrange("p (t c) -> p t c", c=GC),
                                       mask, ALU.mult).then_inc(self.sem("ls"), 1)

    def tensor(self, pe):
        k = self.k
        mm = pe.matmul
        with pe.Fori(0, self.iters) as i:
            for lane in self.lanes():
                self.wait(pe, "rows", self.count(i, lane))
                mm(self.bank(lane, 0), k.ones[0:GH, :], self.gm[lane], start=True, stop=True)
                mm(self.bank(lane, 1), k.ones[0:GH, :], self.bm[lane], start=True, stop=True).then_inc(self.sem("bcast"), 1)
            for lane in self.lanes():
                for n, of in enumerate((self.kT, self.vT)):
                    self.wait(pe, "kv", i * 4 + (lane * 2 + n + 1))
                    for t in range(GCN):
                        ins = pe.transpose(self.bank(lane, 2 + n, t), of[lane][:, chunk_at(t)], k.ident[:])
                ins.then_inc(self.sem("turned"), 1)
            for lane in self.lanes():
                self.wait(pe, "masked", self.count(i, lane))
                for t in range(GCN):
                    kt = self.kT[lane][:, chunk_at(t)]
                    mm(self.bank(lane, 0, t), kt, kt, start=True, stop=True)
                for t in range(GCN):
                    ins = mm(self.bank(lane, 1, t), self.kT[lane][:, chunk_at(t)], self.tile(0, i, lane)[:, chunk_at(t)], start=True, stop=True)
                ins.then_inc(self.sem("gram"), 1)
            for l in range(LEVELS):
                for lane in self.lanes():
                    self.wait(pe, "ls", self.count(i, lane, l, LEVELS))
                    if l > 0:
                        self.wait(pe, "x", self.count(i, lane, l - 1, LEVELS))
                    for t in range(GCN):
                        rhs = k.ident[:] if l == 0 else self.X[lane][:, chunk_at(t)]
                        ins = mm(self.bank(lane, 0, t), self.Ls[lane][:, chunk_at(t)], rhs, start=True, stop=True)
                    ins.then_inc(self.sem("t1"), 1)
                if l == 0:
                    continue
                for lane in self.lanes():
                    self.wait(pe, "t1_copied", self.count(i, lane, l - 1, LEVELS - 1))
                    for t in range(GCN):
                        if l < LEVELS - 1:
                            mm(self.bank(lane, 1, t), self.XT[lane][:, chunk_at(t)], self.T1[lane][:, chunk_at(t)], start=True, stop=True)
                        ins = mm(self.bank(lane, 2, t), self.T1[lane][:, chunk_at(t)], self.XT[lane][:, chunk_at(t)], start=True, stop=True)
                    ins.then_inc(self.sem("dx"), 1)
            for lane in self.lanes():
                self.wait(pe, "x", self.count(i, lane, LEVELS - 1, LEVELS))
                for t in range(GCN):
                    ins = mm(self.bank(lane, 3, t), self.kb[lane][:, chunk_at(t)], self.XT[lane][:, chunk_at(t)], start=True, stop=True)
                ins.then_inc(self.sem("w"), 1)
            for t in range(GCN):
                for lane in self.lanes():
                    out = self.bank(lane, 0, t)
                    if t == 1:
                        self.wait(pe, "w_copied", self.count(i, lane))
                    if t > 0:
                        self.wait(pe, "s", self.count(i, lane, t - 1, GCN - 1))
                    ins = mm(out, self.XT[lane][:, chunk_at(t)], self.vb[lane][:, chunk_at(t)], start=True, stop=(t == 0))
                    if t > 0:
                        ins = mm(out, self.wT[lane][:, chunk_at(t)], self.S[lane], start=False, stop=True)
                    ins.then_inc(self.sem("vn"), 1)
                for lane in self.lanes():
                    self.wait(pe, "new", self.count(i, lane, t, GCN))
                    new = self.new[lane][:, t % 2]
                    if t > 0:
                        mm(self.bank(lane, 2, t), self.S[lane], self.qe[lane][:, chunk_at(t)], start=True, stop=False)
                    ins = mm(self.bank(lane, 2, t), new, self.qk[lane][:, chunk_at(t)], start=(t == 0), stop=True)
                    if t == GCN - 1:
                        ins.then_inc(self.sem("o"), 1)
                    else:
                        mm(self.bank(lane, 3, t), self.kd[lane][:, chunk_at(t)], new, start=True, stop=True).then_inc(self.sem("s_add"), 1)

    def scalar(self, act):
        din = self.din
        with act.Fori(0, self.iters) as i:
            for lane in self.lanes():
                self.wait(act, "bcast", self.count(i, lane))
                act.activation(self.eg[lane], self.bank(lane, 0), ACT.Exp).then_inc(self.sem("eg"), 1)
                self.wait(act, "diff", self.count(i, lane))
                act.activation(self.decay[lane], self.decay[lane], ACT.Exp)
                act.activation(self.kdx[lane], self.kdx[lane], ACT.Exp).then_inc(self.sem("exp"), 1)
            for lane in self.lanes():
                self.wait(act, "turned", self.count(i, lane))
                for t in range(GCN):
                    beta = din.colm[:, 1, t, bass.ds(i * self.LANES + lane, 1)]
                    ins = act.activation(self.vb[lane][:, chunk_at(t)], self.bank(lane, 3, t), ACT.Identity, scale=beta)
                ins.then_inc(self.sem("vb"), 1)
            for l in range(1, LEVELS):
                for lane in self.lanes():
                    self.wait(act, "t1", self.count(i, lane, l, LEVELS))
                    act.activation(self.T1[lane], self.bank(lane, 0), ACT.Copy).then_inc(self.sem("t1_copied"), 1)
            for lane in self.lanes():
                self.wait(act, "w", self.count(i, lane))
                act.activation(self.wT[lane], self.bank(lane, 3), ACT.Copy).then_inc(self.sem("w_copied"), 1)
            for t in range(GCN):
                for lane in self.lanes():
                    self.wait(act, "vn", self.count(i, lane, t, GCN))
                    act.activation(self.new[lane][:, t % 2], self.bank(lane, 0, t), ACT.Copy).then_inc(self.sem("new"), 1)
            for lane in self.lanes():
                self.wait(act, "o", self.count(i, lane))
                act.activation(self.tile(0, i, lane), self.bank(lane, 2), ACT.Copy).then_inc(self.sem("lane_free"), 1)

    STEPS = 2 * 3

    def vector(self, dve, st):
        k, din = self.k, self.din
        by_chunk = lambda ap: ap.rearrange("p (t c) -> p t c", c=GC)
        each = lambda m: m.unsqueeze(1).to_broadcast([P, GCN, GC])
        with dve.Fori(0, self.iters) as i:
            st.enter(i, self.STEPS)
            head = lambda lane: bass.ds(i * self.LANES + lane, 1)
            for lane in self.lanes():
                self.wait(dve, "lane_free", self.count(i, lane))
                mine = k.ident[0:GH, head(lane)]
                dve.tensor_scalar(self.gm[lane], din.g_rows, mine, None, ALU.mult)
                dve.tensor_scalar(self.bm[lane], din.b_rows, mine, None, ALU.mult).then_inc(self.sem("rows"), 1)
            for lane in self.lanes():
                self.wait(dve, "eg", self.count(i, lane))
                for t in range(GCN):
                    dve.tensor_scalar(self.decay[lane][:, chunk_at(t)], self.bank(lane, 0, t), din.colm[:, 0, t, head(lane)], 0.0, ALU.subtract, ALU.min)
                last = by_chunk(self.bank(lane, 0))[:, :, GC - 1:GC]
                dve.tensor_tensor(self.kdx[lane].unsqueeze(2), last, din.colm[:, 0, :, head(lane)], ALU.subtract).then_inc(self.sem("diff"), 1)
            for lane in self.lanes():
                self.wait(dve, "exp", self.count(i, lane))
                dve.tensor_tensor(self.qe[lane], self.eg[lane], self.tile(0, i, lane), ALU.mult)
                a = st.done(dve.tensor_tensor(by_chunk(self.LT[lane]), by_chunk(self.decay[lane]), each(din.strict), ALU.mult))
                st.wait(a)
                st.done(dve.tensor_tensor(by_chunk(self.decay[lane]), by_chunk(self.decay[lane]), each(din.upper), ALU.mult))
                dve.tensor_tensor(self.LT[lane], self.LT[lane], self.bank(lane, 1), ALU.mult).then_inc(self.sem("masked"), 1)
            for lane in self.lanes():
                self.wait(dve, "turned", self.count(i, lane))
                for t in range(GCN):
                    dve.tensor_scalar(self.kb[lane][:, chunk_at(t)], self.bank(lane, 2, t), din.colm[:, 2, t, head(lane)], None, ALU.mult)
                    ins = dve.tensor_scalar(self.kd[lane][:, chunk_at(t)], self.bank(lane, 2, t), self.kdx[lane][:, t:t + 1], None, ALU.mult)
                st.done(ins)
            for lane in self.lanes():
                self.wait(dve, "gram", self.count(i, lane))
                self.wait(dve, "masked", self.count(i, lane))
                dve.tensor_tensor(self.qk[lane], self.decay[lane], self.bank(lane, 1), ALU.mult)
                dve.tensor_tensor(self.LT[lane], self.LT[lane], self.bank(lane, 0), ALU.mult).then_inc(self.sem("lt"), 1)
            for l in range(LEVELS):
                for lane in self.lanes():
                    XT, X = self.XT[lane], self.X[lane]
                    if l == 0:
                        self.wait(dve, "t1", self.count(i, lane, 0, LEVELS))
                        dve.tensor_tensor(by_chunk(X), each(k.ident[:]), by_chunk(self.bank(lane, 0)), ALU.subtract)
                        ins = dve.tensor_tensor(by_chunk(XT), each(k.ident[:]), by_chunk(self.Ls[lane]), ALU.subtract)
                    else:
                        self.wait(dve, "dx", self.count(i, lane, l - 1, LEVELS - 1))
                        if l < LEVELS - 1:
                            dve.tensor_tensor(X, X, self.bank(lane, 1), ALU.subtract)
                        ins = dve.tensor_tensor(XT, XT, self.bank(lane, 2), ALU.subtract)
                    ins.then_inc(self.sem("x"), 1)
            for t in range(GCN - 1):
                for lane in self.lanes():
                    self.wait(dve, "s_add", self.count(i, lane, t, GCN - 1))
                    add, S = self.bank(lane, 3, t), self.S[lane]
                    if t == 0:
                        ins = dve.tensor_copy(S, add)
                    else:
                        self.wait(dve, "s", self.count(i, lane, t - 1, GCN - 1))
                        ins = dve.scalar_tensor_tensor(S, S, self.eg[lane][:, (t + 1) * GC - 1:(t + 1) * GC], add, ALU.mult, ALU.add)
                    ins.then_inc(self.sem("s"), 1)
            st.leave(self.iters)



class ResidualNorm(Signals):

    BANKS = 4

    def __init__(self, k, stream, weight, kt, per, source, room, layer, gate, norm, after):
        super().__init__(k, "residual", added=self.BANKS + KD, mean=1, rooted=2, squared=KD, var=KD, centred=KD, scaled=KD, normed=KD, modulated=KD)
        self.stream, self.weight, self.kt, self.per = stream, weight, kt, per
        self.source, self.layer, self.gate, self.norm, self.after = source, layer, gate, norm, after
        self.square = room.take(2, T)
        self.inv = room.take(T)
        self.chunks = KD // per
        self.upper = room.take(2, kt * per * P)
        self.input = SplitInput(k, kt, source, room)

    def sync(self, sp):
        self.stream.load_run(sp, [self.weight], self.kt, self.per * P, self.chunks)

    def tensor(self, pe, stream):
        k = self.k
        pe.sem_inc(self.sem("added"), self.BANKS)

        def chunk(n, i, c):
            stream.split_landed(pe, n, i, c)
            lower, upper = stream.lower(n, self.kt, self.per * P), stream.upper(self.upper, n, self.kt, self.per * P)
            for f in range(self.per):
                j = c * self.per + f
                self.wait(pe, "added", i * (NSLOT * self.per) + (j + 1))
                at = slice(f * P, (f + 1) * P)
                ins = self.input.products(pe, k.ps[:, j % self.BANKS, :], upper[:, :, at], lower[:, :, at], c == 0 and f == 0)
                stream.group_done(ins, f == self.per - 1)

        stream.rounds(pe, self.chunks, self.per, chunk, True)
        self.wait(pe, "added", self.BANKS + KD)
        for j in range(KD):
            ins = pe.matmul(k.ps[:, 6, :], k.mean[:], k.xT[:, j, :], start=(j == 0), stop=(j == KD - 1))
        ins.then_inc(self.sem("mean"), 1)
        for j in range(KD):
            self.wait(pe, "squared", j + 1)
            pe.matmul(k.ps[:, 7, :], k.mean[:], self.square[:, j % 2], start=(j == 0), stop=(j == KD - 1)).then_inc(self.sem("var"), 1)

    def vector(self, dve, st, stream):
        k = self.k

        def add(n, i, c):
            for f in range(self.per):
                j = c * self.per + f
                stream.wait_group(dve, n, i, c, f)
                at = i * (NSLOT * self.per) + j
                x = k.xT[:, bass.ds(at, 1), :].rearrange("p o t -> p (o t)")
                dve.scalar_tensor_tensor(x, k.ps[:, j % self.BANKS, :], k.mod[:, self.layer, self.gate, bass.ds(at, 1)], x, ALU.mult, ALU.add)\
                   .then_inc(self.sem("added"), 1)

        self.input.vector(dve)
        stream.rounds(dve, self.chunks, self.per, add, True)
        self.wait(dve, "mean", 1)
        self.wait(dve, "added", self.BANKS + KD)
        for j in range(KD):
            dve.tensor_tensor(k.xT[:, j, :], k.xT[:, j, :], k.ps[:, 6, :], ALU.subtract).then_inc(self.sem("centred"), 1)
        self.wait(dve, "rooted", 2)
        for j in range(KD):
            self.wait(dve, "squared", KD)
            dve.tensor_tensor(k.xT[:, j, :], k.xT[:, j, :], self.inv, ALU.mult).then_inc(self.sem("scaled"), 1)
        if self.after:
            for j in range(KD):
                self.wait(dve, "modulated", j + 1)
                dve.tensor_scalar(k.xT[:, j, :], k.xT[:, j, :], ALPHA, None, ALU.mult)

    def scalar(self, act, stream):
        k = self.k
        for c in range(self.chunks):
            stream.round_chunk(act, self.upper, stream.n + c, 0, self.kt, self.per * P)
            if c == 0:
                self.input.scalar(act)
        stream.skip(self.chunks, self.per, True)
        l, b = self.layer, self.norm
        for j in range(KD):
            self.wait(act, "centred", j + 1)
            if j >= 2:
                self.wait(act, "var", j - 1)
            act.activation(self.square[:, j % 2], k.xT[:, j, :], ACT.Square).then_inc(self.sem("squared"), 1)
        self.wait(act, "var", KD)
        act.activation(self.inv, k.ps[:, 7, :], ACT.Ln, bias=k.eps[:, 0:1]).then_inc(self.sem("rooted"), 1)
        self.wait(act, "rooted", 1)
        act.activation(self.inv, self.inv, ACT.Exp, scale=-0.5).then_inc(self.sem("rooted"), 1)
        for j in range(KD):
            self.wait(act, "scaled", j + 1)
            act.activation(k.xT[:, j, :], k.xT[:, j, :], ACT.Identity, bias=k.col("ln_b", (2 * l + b) * KD + j),
                           scale=k.col("ln_g", (2 * l + b) * KD + j)).then_inc(self.sem("normed"), 1)
            if self.after and j:
                self.modulate(act, j - 1)
        if self.after:
            self.modulate(act, KD - 1)

    def modulate(self, act, j):
        k, (la, m) = self.k, self.after
        self.wait(act, "normed", j + 1)
        act.activation(k.hT[:, j, 0:T], k.xT[:, j, :], ACT.Identity, bias=k.mod[:, la, m, j:j + 1],
                       scale=k.mod[:, la, m + 1, j:j + 1]).then_inc(self.sem("modulated"), 1)

    def gpsimd(self, pool, stream):
        k = self.k
        stream.lower_chunks(pool, self.upper, self.chunks, self.per, self.kt, self.per * P)



class FeedForwardUp(Signals):

    CHUNKS = 2 * FT // 2

    def __init__(self, k, stream, layer):
        super().__init__(k, "ffn", convolved=2 + FT, acted=2 + FT, silu=2 + FT)
        self.stream, self.layer = stream, layer
        room = Room(k.arena)
        self.acts = room.take(FT, T)
        self.pre = room.take(2, T)
        self.gate = room.take(2, T)
        self.room = Room(k.arena[:, FT * T:])
        room = Room(k.arena[:, room.regions[0][1]:])
        self.upper = room.take(2, KD * 2 * P)
        self.input = SplitInput(k, KD, lambda r: k.hT[:, r, 0:T], room)
        self.next = NextConditioning(k, room) if layer == 0 else None

    def sync(self, sp):
        w = tiles_of(self.k.ins["ffn_up"][self.layer])
        self.stream.load_run(sp, [w[:, :, 0:F], w[:, :, F:2 * F]], KD, 2 * P, self.CHUNKS, self.beside(self.next.sync, sp) if self.next else None)

    def beside(self, part, *to):
        def at(i, c):
            if not isinstance(i, int):
                if c % 2:
                    part(*to, i, c // 2)
            else:
                part(*to, c // NSLOT, c % NSLOT)
        assert self.CHUNKS % NSLOT == 2 and self.CHUNKS // NSLOT * 2 + 2 == NextConditioning.COUNT
        return at

    def at(self, i, c, f):
        return i * NSLOT, 2 * (c // 2) + f

    def tensor(self, pe, stream):
        k = self.k
        pe.sem_inc(self.sem("convolved"), 2)
        pe.sem_inc(self.sem("acted"), 2)

        def chunk(n, i, c):
            stream.split_landed(pe, n, i, c)
            lower, upper = stream.lower(n, KD, 2 * P), stream.upper(self.upper, n, KD, 2 * P)
            for f in range(2):
                part, j = self.at(i, c, f)
                self.wait(pe, ("convolved", "acted")[c % 2], part + (j + 1))
                at = slice(f * P, (f + 1) * P)
                ins = self.input.products(pe, k.ps[:, 2 * (c % 2) + f, :], upper[:, :, at], lower[:, :, at], c == 0 and f == 0)
                stream.group_done(ins, f == 1)
            if self.next:
                beside(i, c)

        beside = self.beside(self.next.tensor, pe) if self.next else None
        stream.rounds(pe, self.CHUNKS, 2, chunk, True)

    def vector(self, dve, st, stream):
        k, l = self.k, self.layer
        dve.sem_inc(self.sem("silu"), 2)

        def chunk(n, i, c):
            looped = not isinstance(i, int)
            if c == 0 and looped:
                st.enter(i, NSLOT * (FFN_CONV - 1) + (2 * (KD - 1) if self.next else 0))
            if self.next:
                beside(i, c)
            for f in range(2):
                part, j = self.at(i, c, f)
                stream.wait_group(dve, n, i, c, f)
                src = k.ps[:, 2 * (c % 2) + f, :]
                if c % 2 == 0:
                    self.wait(dve, "silu", part + (j + 1))
                    pre = self.pre[:, f]
                    for back in range(FFN_CONV):
                        w = k.col("ffn_conv_w", part + ((l * FFN_CONV + FFN_CONV - 1 - back) * FT + j))
                        if back == 0:
                            st.done(dve.tensor_scalar(pre, src, w, None, ALU.mult))
                            continue
                        st.wait()
                        ins = dve.scalar_tensor_tensor(pre[:, back:], src[:, 0:T - back], w, pre[:, back:], ALU.mult, ALU.add)
                        if back < FFN_CONV - 1:
                            st.done(ins)
                    ins.then_inc(self.sem("convolved"), 1)
                else:
                    self.wait(dve, "silu", part + (j + 3))
                    out = self.acts[:, bass.ds(part + j, 1), :].rearrange("p o t -> p (o t)")
                    dve.tensor_tensor(out, self.gate[:, f], src, ALU.mult).then_inc(self.sem("acted"), 1)
            if c == NSLOT - 1 and looped:
                st.leave(self.CHUNKS // NSLOT)

        beside = self.beside(self.next.vector, dve, st) if self.next else None
        self.input.vector(dve)
        stream.rounds(dve, self.CHUNKS, 2, chunk, True)
        if self.next:
            self.next.finish(dve, st)

    def scalar(self, act, stream):
        k, l = self.k, self.layer

        def chunk(n, i, c):
            if not isinstance(i, int) or c + 1 < self.CHUNKS:
                stream.round_chunk(act, self.upper, n + 1, i, KD, 2 * P)
            if c % 2:
                return
            for f in range(2):
                part, j = self.at(i, c, f)
                self.wait(act, "convolved", part + (j + 3))
                self.wait(act, "acted", part + (j + 1))
                act.activation(self.gate[:, f], self.pre[:, f], ACT.Silu, bias=k.col("ffn_conv_b", part + (l * FT + j))).then_inc(self.sem("silu"), 1)

        assert self.CHUNKS % NSLOT
        stream.round_chunk(act, self.upper, stream.n, 0, KD, 2 * P)
        self.input.scalar(act)
        stream.rounds(act, self.CHUNKS, 2, chunk, True)

    def gpsimd(self, pool, stream):
        stream.lower_chunks(pool, self.upper, self.CHUNKS, 2, KD, 2 * P)



class RetentionIn:

    RUN = KD

    def __init__(self, k, stream):
        self.k, self.stream = k, stream
        room = Room(k.arena)
        self.qk = room.take(2 * KD, T)
        self.v = room.take(TT, RH * R_DV)
        self.gate = room.take(2 * KD, T)
        self.rest = k.arena[:, room.regions[0][1]:]
        room = Room(self.rest)
        self.rope = room.take(2, T)
        self.tmp = room.take(2, T)

    def sync(self, sp):
        k = self.k
        k.stage_over(sp, 9)
        k.load_tables(sp, "rope", [(self.rope, k.tables["t_rope"])])
        self.stream.load_run(sp, [tiles_of(k.ins["ret_w_in"])], KD, 2 * P, 3 * self.RUN)

    def tensor(self, pe, stream):
        k = self.k
        pe.sem_inc(k.sem("ret_rotated"), 2)
        pe.sem_inc(k.sem("ret_v_copied"), TT)
        pe.sem_inc(k.sem("ret_gated"), 4)

        def features(freed, per_chunk):
            def chunk(n, i, c):
                stream.landed(pe, n, i)
                w = stream.slot(n, KD, 2 * P)
                for f in range(2):
                    g = 2 * c + f
                    if per_chunk == 1 and f == 0:
                        pe.wait_ge(k.sem(freed), i * NSLOT + (c + 1))
                    elif per_chunk == 2:
                        pe.wait_ge(k.sem(freed), i * (2 * NSLOT) + (g + 1))
                    for r in range(KD):
                        ins = pe.matmul(k.ps[:, g % 4, :], w[:, r, f * P:(f + 1) * P], k.hT[:, r, 0:T],
                                        start=(r == 0), stop=(r == KD - 1))
                    stream.group_done(ins, f == 1)
            return chunk

        def tokens(n, i, c):
            stream.landed(pe, n, i)
            w = stream.slot(n, KD, 2 * P)
            for t in range(TT):
                pe.wait_ge(k.sem("ret_v_copied"), i * (TT * NSLOT) + (TT * c + t + 1))
                for r in range(KD):
                    ins = pe.matmul(k.ps[:, 4 + t, 0:2 * P], k.hT[:, r, t * P:(t + 1) * P], w[:, r, :],
                                    start=(r == 0), stop=(r == KD - 1))
                stream.group_done(ins, t == TT - 1)

        stream.rounds(pe, self.RUN, 2, features("ret_rotated", 1))
        stream.rounds(pe, self.RUN, TT, tokens)
        pe.wait_ge(k.sem("ret_rotated"), 2 + self.RUN)
        stream.rounds(pe, self.RUN, 2, features("ret_gated", 2))

    def vector(self, dve, st, stream):
        k = self.k
        k.wait_tables(dve, "rope")
        cos, sin = self.rope[:, 0, :], self.rope[:, 1, :]

        def chunk(n, i, c):
            if c == 0:
                st.enter(i, 3 * NSLOT)
            stream.wait_group(dve, n, i, c, 1)
            a, b = k.ps[:, (2 * c) % 4, :], k.ps[:, (2 * c + 1) % 4, :]
            to = lambda f: self.qk[:, bass.ds(i * (2 * NSLOT) + (2 * c + f), 1), :].rearrange("p o t -> p (o t)")
            dve.tensor_tensor(to(0), a, cos, ALU.mult)
            dve.tensor_tensor(to(1), a, sin, ALU.mult)
            dve.tensor_tensor(self.tmp[:, 0], b, sin, ALU.mult)
            st.done(dve.tensor_tensor(self.tmp[:, 1], b, cos, ALU.mult))
            st.wait()
            st.done(dve.tensor_tensor(to(0), to(0), self.tmp[:, 0], ALU.subtract))
            st.done(dve.tensor_tensor(to(1), to(1), self.tmp[:, 1], ALU.add))
            st.wait()
            dve.nop().then_inc(k.sem("ret_rotated"), 1)
            if c == NSLOT - 1:
                st.leave(self.RUN // NSLOT)

        stream.rounds(dve, self.RUN, 2, chunk)
        stream.skip(self.RUN, TT)
        stream.skip(self.RUN, 2)

    def scalar(self, act, stream):
        k = self.k
        stream.skip(self.RUN, 2)

        def tokens(n, i, c):
            for t in range(TT):
                stream.wait_group(act, n, i, c, t)
                act.activation(self.v[:, t, bass.ds(i * (2 * P * NSLOT) + 2 * P * c, 2 * P)], k.ps[:, 4 + t, 0:2 * P], ACT.Copy)\
                   .then_inc(k.sem("ret_v_copied"), 1)

        def gate(n, i, c):
            for f in range(2):
                stream.wait_group(act, n, i, c, f)
                g = 2 * c + f
                to = self.gate[:, bass.ds(i * (2 * NSLOT) + g, 1), :].rearrange("p o t -> p (o t)")
                act.activation(to, k.ps[:, g % 4, :], ACT.Silu).then_inc(k.sem("ret_gated"), 1)

        stream.rounds(act, self.RUN, TT, tokens)
        stream.rounds(act, self.RUN, 2, gate)

    def gpsimd(self, pool, stream):
        stream.skip(self.RUN, 2)
        stream.skip(self.RUN, TT)
        stream.skip(self.RUN, 2)



class RetentionHeads(Signals):

    def __init__(self, k, rin):
        super().__init__(k, "heads", masked=RH * TT, o=R_VT + RH * R_VT, scored=TT + RH * TT, o_copied=RH * R_VT)
        self.rin = rin
        room = Room(rin.rest, k.hT[:].rearrange("p j t -> p (j t)"))
        self.key = room.take(2, T)
        self.scores = [room.take(T - P * j) for j in range(TT)]
        self.o = room.take(R_VT, T)
        self.square = room.take(2, T)
        self.inv = room.take(T)
        self.decay = room.take(RH, T)
        self.val = room.take(TT, R_DV)

    def sync(self, sp):
        k = self.k
        k.stage_over(sp, 10)
        k.load_tables(sp, "decay", [(self.decay, k.tables["t_decay"])])

    def gpsimd(self, pool):
        pool.sem_inc(self.sem("scored"), TT)
        pool.sem_inc(self.sem("o"), R_VT)
        with pool.Fori(0, RH) as i:
            self.wait(pool, "scored", i * TT + TT)
            for f in range(2):
                src = self.rin.qk[:, bass.ds(i * 2 + (KD + f), 1), :].rearrange("p o t -> p (o t)")
                ins = pool.tensor_copy(self.key[:, f], src)
            ins.then_inc(self.sem("key"), 1)
            self.wait(pool, "o", i * R_VT + R_VT)
            for t in range(TT):
                ins = pool.tensor_copy(self.val[:, t], self.rin.v[:, t, bass.ds(i * R_DV, R_DV)])
            ins.then_inc(self.sem("val"), 1)

    def tensor(self, pe):
        k = self.k
        pe.sem_inc(self.sem("head"), 1)
        with pe.Fori(0, RH) as i:
            self.wait(pe, "key", i + 1)
            for j in range(TT):
                for f in range(2):
                    q = self.rin.qk[:, bass.ds(i * 2 + f, 1), :].rearrange("p o t -> p (o t)")
                    ins = pe.matmul(k.ps[:, j, 0:T - P * j], self.key[:, f, j * P:(j + 1) * P], q[:, j * P:T], start=(f == 0), stop=(f == 1))
                ins.then_inc(self.sem("scored"), 1)
            self.wait(pe, "val", i + 1)
            self.wait(pe, "head", i + 1)
            self.wait(pe, "masked", i * TT + TT)
            for m in range(R_VT):
                for j in range(TT):
                    ins = pe.matmul(k.ps[:, 4 + m, P * j:T], self.val[:, j, m * P:(m + 1) * P], self.scores[j], start=(j == 0), stop=(j == TT - 1))
                ins.then_inc(self.sem("o"), 1)
            for m in range(R_VT):
                self.wait(pe, "o_copied", i * R_VT + (R_VT if m == 0 else m + 1))
                ins = pe.matmul(k.ps[:, 4, :], k.mean[:], self.o[:, m], start=(m == 0), stop=(m == R_VT - 1))
            ins.then_inc(self.sem("mean"), 1)
            for m in range(R_VT):
                self.wait(pe, "squared", i * R_VT + (m + 1))
                pe.matmul(k.ps[:, 5, :], k.mean[:], self.square[:, m % 2], start=(m == 0), stop=(m == R_VT - 1)).then_inc(self.sem("var"), 1)

    SCALE = D / R_DV

    def vector(self, dve, st):
        k = self.k
        k.wait_tables(dve, "decay")
        with dve.Fori(0, RH) as i:
            st.enter(i, R_VT)
            for j in range(TT):
                self.wait(dve, "scored", i * TT + (TT + j + 1))
                if j == 0:
                    self.wait(dve, "o", i * R_VT + R_VT)
                decay = self.decay[:, bass.ds(i, 1), 0:T - P * j].rearrange("p o t -> p (o t)")
                dve.tensor_tensor(self.scores[j], k.ps[:, j, 0:T - P * j], decay, ALU.mult).then_inc(self.sem("masked"), 1)
            self.wait(dve, "mean", i + 1)
            for m in range(R_VT):
                dve.scalar_tensor_tensor(self.o[:, m], k.ps[:, 4, :], -self.SCALE, self.o[:, m], ALU.mult, ALU.add).then_inc(self.sem("centred"), 1)
            self.wait(dve, "rooted", i * 2 + 2)
            self.wait(dve, "centred", i * R_VT + R_VT)
            for m in range(R_VT):
                st.done(dve.tensor_tensor(self.o[:, m], self.o[:, m], self.inv, ALU.mult))
            for m in range(R_VT):
                st.wait(st.n - R_VT + m + 1)
                gate = self.rin.gate[:, bass.ds(i * R_VT + m, 1), :].rearrange("p o t -> p (o t)")
                ins = dve.tensor_tensor(gate, self.o[:, m], gate, ALU.mult)
            ins.then_inc(self.sem("head"), 1)
            st.leave(RH)

    def scalar(self, act):
        k = self.k
        act.sem_inc(self.sem("var"), 2)
        with act.Fori(0, RH) as i:
            for m in range(R_VT):
                self.wait(act, "o", i * R_VT + (R_VT + m + 1))
                if m == 0:
                    self.wait(act, "head", i + 1)
                act.activation(self.o[:, m], k.ps[:, 4 + m, :], ACT.Copy).then_inc(self.sem("o_copied"), 1)
            for m in range(R_VT):
                self.wait(act, "centred", i * R_VT + (m + 1))
                self.wait(act, "var", i * R_VT + (m + 1))
                act.activation(self.square[:, m % 2], self.o[:, m], ACT.Square).then_inc(self.sem("squared"), 1)
            self.wait(act, "var", i * R_VT + (R_VT + 2))
            act.activation(self.inv, k.ps[:, 5, :], ACT.Ln, bias=k.eps[:, 1:2], scale=self.SCALE).then_inc(self.sem("rooted"), 1)
            self.wait(act, "rooted", i * 2 + 1)
            act.activation(self.inv, self.inv, ACT.Exp, scale=-0.5).then_inc(self.sem("rooted"), 1)



class FeatureNorm(Signals):

    def __init__(self, k, room, nt, source, out, gain, parts):
        super().__init__(k, "norm", squared=nt, summed=nt, rooted=len(parts) + 1)
        self.nt, self.source, self.out, self.gain, self.parts = nt, source, out, gain, parts
        width = parts[-1].stop
        self.square = room.take(2, width)
        self.inv = room.take(width)

    def scalar(self, act):
        k = self.k
        for j in range(self.nt):
            if j >= 2:
                self.wait(act, "summed", j - 1)
            act.activation(self.square[:, j % 2], self.source(j), ACT.Square).then_inc(self.sem("squared"), 1)
        self.wait(act, "summed", self.nt)
        for n, part in enumerate(self.parts):
            act.activation(self.inv[:, part], k.ps[:, 6 + n, 0:part.stop - part.start], ACT.Ln, bias=k.eps[:, 1:2], scale=KD / self.nt)\
               .then_inc(self.sem("rooted"), 1)
        self.wait(act, "rooted", len(self.parts))
        act.activation(self.inv, self.inv, ACT.Exp, scale=-0.5).then_inc(self.sem("rooted"), 1)

    def tensor(self, pe):
        k = self.k
        for j in range(self.nt):
            self.wait(pe, "squared", j + 1)
            for n, part in enumerate(self.parts):
                ins = pe.matmul(k.ps[:, 6 + n, 0:part.stop - part.start], k.mean[:], self.square[:, j % 2, part], start=(j == 0), stop=(j == self.nt - 1))
            ins.then_inc(self.sem("summed"), 1)

    def vector(self, dve, st):
        self.wait(dve, "rooted", len(self.parts) + 1)
        for j in range(self.nt):
            dve.scalar_tensor_tensor(self.out(j), self.source(j), self.gain(j), self.inv, ALU.mult, ALU.mult)

    def gpsimd(self, pool):
        pass


class Prepend:

    def __init__(self, k, gates):
        self.k, self.runs = k, gates.runs
        self.meta = Room(k.arena[:, 24576:]).take(D)[0:N_META]

    def sync(self, sp):
        k = self.k
        k.stage_over(sp, k.base)
        k.load_tables(sp, "meta", [(self.meta, k.ins["meta_tokens_2"]), (self.runs, k.tables["t_runs"])])

    def tensor(self, pe):
        k = self.k
        k.wait_tables(pe, "meta")
        for j in range(KD):
            ins = pe.transpose(k.ps[:, 0, j * N_META:(j + 1) * N_META], self.meta[:, j * P:(j + 1) * P], k.ident[0:N_META, 0:N_META])
        ins.then_inc(k.sem("meta_turned"), 1)

    def vector(self, dve):
        k = self.k
        dve.wait_ge(k.sem("meta_turned"), 1)
        dve.tensor_copy(k.hT[:, :, 0:N_META], k.ps[:, 0, 0:KD * N_META].rearrange("p (j t) -> p j t", j=KD))

    def scalar(self, act):
        k = self.k
        for j in range(KD):
            act.activation(k.hT[:, j, N_META:], k.xT[:, j, :], ACT.Copy)

    def gpsimd(self, pool):
        pass


class MixerIn(Signals):

    def __init__(self, k, stream, tiles, first, chunks, room, input, splits_input):
        super().__init__(k, "mixer_in", copied=4 + 2 * chunks)
        self.stream, self.tiles, self.first, self.chunks = stream, tiles, first, chunks
        self.upper = room.take(2, KD * 2 * P)
        self.input, self.splits_input = input, splits_input

    def sync(self, sp):
        w = tiles_of(self.k.ins["w_in_2"])[:, :, self.first:self.first + self.chunks * 2 * P]
        self.stream.load_run(sp, [w], KD, 2 * P, self.chunks)

    def tensor(self, pe, stream):
        k = self.k
        pe.sem_inc(self.sem("copied"), 4)

        def chunk(n, i, c):
            stream.split_landed(pe, n, i, c)
            lower, upper = stream.lower(n, KD, 2 * P), stream.upper(self.upper, n, KD, 2 * P)
            for f in range(2):
                g = 2 * c + f
                at = slice(f * P, (f + 1) * P)
                self.wait(pe, "copied", i * (2 * NSLOT) + (g + 1))
                for half, part in enumerate((slice(0, HALF), slice(HALF, L2))):
                    ins = self.input.products(pe, k.ps[:, 2 * (g % 4) + half, 0:HALF], upper[:, :, at], lower[:, :, at],
                                              self.splits_input and g == 0 and half == 0, part)
                stream.group_done(ins, f == 1)

        stream.rounds(pe, self.chunks, 2, chunk, True)

    def scalar(self, act, stream):
        k = self.k

        def chunk(n, i, c):
            if not isinstance(i, int) or c + 1 < self.chunks:
                stream.round_chunk(act, self.upper, n + 1, i, KD, 2 * P)
            for f in range(2):
                g = 2 * c + f
                stream.wait_group(act, n, i, c, f)
                to = self.tiles[:, bass.ds(i * (2 * NSLOT) + g, 1), :].rearrange("p o (a t) -> p (o a) t", a=2)
                act.activation(to, k.ps[:, 2 * (g % 4):2 * (g % 4) + 2, 0:HALF], ACT.Copy).then_inc(self.sem("copied"), 1)

        assert self.chunks % NSLOT
        stream.round_chunk(act, self.upper, stream.n, 0, KD, 2 * P)
        if self.splits_input:
            self.input.scalar(act)
        stream.rounds(act, self.chunks, 2, chunk, True)

    def vector(self, dve, stream):
        if self.splits_input:
            self.input.vector(dve)
        stream.skip(self.chunks, 2, True)

    def gpsimd(self, pool, stream):
        stream.lower_chunks(pool, self.upper, self.chunks, 2, KD, 2 * P)



class HgrnGates:

    def __init__(self, k):
        self.k = k
        room = Room(k.arena)
        self.tiles = room.take(5 * HYT, L2)
        self.logf = room.take(2 * HYT, L2)
        self.lb = room.take(2, 2, HYT)
        self.runs = room.take(2, L2)
        self.rest = k.arena[:, room.regions[0][1]:ARENA_W - KD * L2]
        self.input_room = Room(k.arena[:, ARENA_W - KD * L2:])

    def vector(self, dve, st):
        k = self.k
        for d, name in enumerate(("lb_fwd_2", "lb_bwd_2")):
            dve.tensor_tensor(self.lb[:, d, 1, :], k.cols(name, 0, HYT), k.cols(name, HYT, HYT), ALU.subtract).then_inc(k.sem("hgrn_lb"), 1)
        dve.wait_ge(k.sem("hgrn_sigmoid"), 2)
        for d in range(2):
            ins = dve.tensor_scalar(self.lb[:, d, 1, :], self.lb[:, d, 0, :], -1.0, 1.0, ALU.mult, ALU.add)
        st.done(ins)
        st.wait()
        for n in range(2 * HYT):
            d, h = divmod(n, HYT)
            f = self.tiles[:, HYT + n, :]
            dve.wait_ge(k.sem("hgrn_sigmoid"), n + 3)
            dve.tensor_scalar(f, f, self.lb[:, d, 1, h:h + 1], self.lb[:, d, 0, h:h + 1], ALU.mult, ALU.add).then_inc(k.sem("hgrn_forget"), 1)
        for n in range(2 * HYT):
            f = self.tiles[:, HYT + n, :]
            dve.wait_ge(k.sem("hgrn_logged"), n + 1)
            dve.tensor_scalar(f, f, -1.0, 1.0, ALU.mult, ALU.add)

    def scalar(self, act):
        k = self.k
        for n in (*range(HYT), *range(4 * HYT, 5 * HYT)):
            act.activation(self.tiles[:, n, :], self.tiles[:, n, :], ACT.Silu)
        act.wait_ge(k.sem("hgrn_lb"), 2)
        for d in range(2):
            act.activation(self.lb[:, d, 0, :], self.lb[:, d, 1, :], ACT.Sigmoid).then_inc(k.sem("hgrn_sigmoid"), 1)
        for n in range(2 * HYT):
            act.activation(self.tiles[:, HYT + n, :], self.tiles[:, HYT + n, :], ACT.Sigmoid).then_inc(k.sem("hgrn_sigmoid"), 1)
        for n in range(2 * HYT):
            act.wait_ge(k.sem("hgrn_forget"), n + 1)
            to = self.logf[:, n, :] if n < HYT else self.logf[:, n, ::-1]
            act.activation(to, self.tiles[:, HYT + n, :], ACT.Ln).then_inc(k.sem("hgrn_logged"), 1)

    def tensor(self, pe):
        pass

    def gpsimd(self, pool):
        pass


class HgrnHeads(Signals):

    PAIRS = T // P

    def __init__(self, k, gates):
        super().__init__(k, "heads", turned=0, masked=0, diff=0, exp=0, o=0, scored=0, o_copied=0)
        self.g = gates
        room = Room(gates.rest)
        two = lambda *shape: [room.take(*shape) for _ in range(2)]
        self.vT = room.take(L2)
        self.b, self.qs, self.ks, self.kd = two(L2), two(T), two(T), two(L2)
        self.vtok = room.take(self.PAIRS + 1, P)
        self.kdtok = two(self.PAIRS + 1, P)
        self.A = two(self.PAIRS, CH)
        self.S = two(NCH, P)
        self.qe = two(T)
        self.dec = two(NCH + 1)

    def tile(self, n, i):
        return self.g.tiles[:, bass.ds(i + n, 1), :].rearrange("p o t -> p (o t)")

    @staticmethod
    def chunks(ap):
        return ap[:, N_META:].rearrange("p (c t) -> p c t", t=CH) if ap.shape[1] == L2 else ap.rearrange("p (c t) -> p c t", t=CH)

    ORDER = [list(range(NCH)), list(range(NCH - 1, -1, -1))]

    @staticmethod
    def quarters(d):
        for row in range(0, P, CH // 2):
            late = row // (CH // 2) % 2
            yield row, row // CH, *((0, CH) if late == d else (0, CH // 2) if d else (CH // 2, CH))

    def added(self, d, n):
        if d == 0 and n == 0:
            return self.k.ps[:, 6, 0:P]
        c = self.ORDER[d][n - 1 if d == 0 else n]
        return self.k.ps[:, 2 * (c % 2) + d, c // 2 * P:(c // 2 + 1) * P]

    def vector(self, dve, st):
        k, g = self.k, self.g
        k.wait_tables(dve, "meta")
        meta = slice(0, N_META)
        with dve.Fori(0, HYT) as i:
            st.enter(i, 2)
            for d in range(2):
                logf = g.logf[:, bass.ds(i + d * HYT, 1), :].rearrange("p o t -> p (o t)")
                runs = g.runs[:, d, :]
                self.wait(dve, "o_copied", i + 1)
                if d == 0:
                    ins = dve.tensor_tensor_scan(self.b[d], runs, logf, 0.0, ALU.mult, ALU.add)
                else:
                    ins = dve.tensor_tensor_scan(self.b[d][:, ::-1], runs, logf, 0.0, ALU.mult, ALU.add)
                ins.then_inc(self.sem("b"), 1)
            for d in range(2):
                self.wait(dve, "b", i * 2 + (d + 1))
                b = self.chunks(self.b[d])
                mid = CH // 2 if d == 0 else CH // 2 - 1
                last = CH - 1 if d == 0 else 0
                dve.tensor_tensor(self.chunks(self.ks[d]), b, b[:, :, mid:mid + 1].to_broadcast([P, NCH, CH]), ALU.subtract)
                if d == 0:
                    dve.tensor_tensor(self.kd[d][:, meta], self.b[d][:, N_META - 1:N_META].to_broadcast([P, N_META]), self.b[d][:, meta], ALU.subtract)
                dve.tensor_tensor(self.chunks(self.kd[d]), b[:, :, last:last + 1].to_broadcast([P, NCH, CH]), b, ALU.subtract).then_inc(self.sem("diff"), 1)
            for d in range(2):
                self.wait(dve, "exp", i * 2 + (d + 1))
                kk, q = self.tile(HYT * (1 + d), i), self.tile(0, i)[:, N_META:]
                if d == 0:
                    dve.tensor_tensor(self.kd[d], self.kd[d], kk, ALU.mult)
                else:
                    dve.tensor_tensor(self.kd[d][:, N_META:], self.kd[d][:, N_META:], kk[:, N_META:], ALU.mult)
                dve.tensor_tensor(self.ks[d], self.ks[d], kk[:, N_META:], ALU.mult)
                dve.tensor_tensor(self.qs[d], self.qs[d], q, ALU.mult)
                dve.tensor_tensor(self.qe[d], self.b[d][:, N_META:], q, ALU.mult).then_inc(self.sem("scaled"), 1)
            for d in range(2):
                order = self.ORDER[d]
                self.wait(dve, "u", i * 2 + (d + 1))
                for n in range(NCH - d):
                    add = self.added(d, n)
                    if n == 0:
                        st.done(dve.tensor_copy(self.S[d][:, 0, :], add))
                        continue
                    if n == 1:
                        st.wait()
                    else:
                        self.wait(dve, "state", i * (2 * NCH - 3) + (d * (NCH - 1) + n - 1))
                    passed = order[n - 1] if d == 0 else order[n]
                    dec = self.dec[d][:, passed:passed + 1]
                    dve.scalar_tensor_tensor(self.S[d][:, n, :], self.S[d][:, n - 1, :], dec, add, ALU.mult, ALU.add).then_inc(self.sem("state"), 1)
            st.leave(HYT)

    def scalar(self, act):
        k = self.k
        with act.Fori(0, HYT) as i:
            for d in range(2):
                self.wait(act, "diff", i * 2 + (d + 1))
                last = CH - 1 if d == 0 else 0
                act.activation(self.qs[d], self.ks[d], ACT.Exp).then_inc(self.sem("e"), 1)
                self.wait(act, "e", i * 4 + (2 * d + 1))
                act.activation(self.ks[d], self.ks[d], ACT.Exp, scale=-1.0)
                part = slice(0 if d == 0 else N_META, L2)
                act.activation(self.kd[d][:, part], self.kd[d][:, part], ACT.Exp)
                act.activation(self.b[d], self.b[d], ACT.Exp).then_inc(self.sem("e"), 1)
                self.wait(act, "e", i * 4 + (2 * d + 2))
                act.activation(self.dec[d][:, 0:NCH].unsqueeze(2), self.chunks(self.b[d])[:, :, last:last + 1], ACT.Copy).then_inc(self.sem("exp"), 1)
            self.wait(act, "turned", i * 3 + 1)
            act.activation(self.vtok[:, 0:self.PAIRS], k.ps[:, 0, :].rearrange("p (n c) -> p n c", c=P), ACT.Copy)
            act.activation(self.vtok[0:N_META, self.PAIRS], k.ps[0:N_META, 1, 0:P], ACT.Copy).then_inc(self.sem("tok"), 1)
            for d in range(2):
                self.wait(act, "turned", i * 3 + (d + 2))
                ins = act.activation(self.kdtok[d][:, 0:self.PAIRS], k.ps[:, 2 + d, :].rearrange("p (n c) -> p n c", c=P), ACT.Copy)
                if d == 0:
                    ins = act.activation(self.kdtok[d][0:N_META, self.PAIRS], k.ps[0:N_META, 6, 0:P], ACT.Copy)
                ins.then_inc(self.sem("tok"), 1)
            for d in range(2):
                self.wait(act, "scored", i * 2 + (d + 1))
                scores = k.ps[:, 4 + d, 0:self.PAIRS * CH].rearrange("p (n c) -> p n c", c=CH)
                for row, _, first, end in self.quarters(d):
                    rows = slice(row, row + CH // 2)
                    ins = act.activation(self.A[d][rows, :, first:end], scores[rows, :, first:end], ACT.Copy)
                ins.then_inc(self.sem("A"), 1)
            self.wait(act, "o", i + 1)
            pairs = lambda ap: ap.rearrange("p (n c t) -> p c n t", c=2, t=CH)
            for half, bank in enumerate((7, 5)):
                ins = act.activation(pairs(self.tile(0, i)[:, 0:T])[:, half], pairs(k.ps[:, bank, :])[:, half], ACT.Copy)
            ins.then_inc(self.sem("o_copied"), 1)

    def gpsimd(self, pool):
        for d in range(2):
            pool.memset(self.A[d], 0.0)
        pool.sem_inc(self.sem("o_copied"), 1)
        for i in range(HYT):
            self.wait(pool, "o_copied", i + 1)
            pool.tensor_copy(self.vT, self.tile(3 * HYT, i)).then_inc(self.sem("v"), 1)
            for d in range(2):
                self.wait(pool, "A", i * 2 + (d + 1))
                sign = 1 if d == 0 else -1
                for half in range(2):
                    part = self.A[d][half * CH:(half + 1) * CH]
                    ins = pool.affine_select(out=part, in_=part, compare_op=ALU.is_ge, fill=0.0, base=0,
                                             pattern=[[0, self.PAIRS], [sign, CH]], channel_multiplier=-sign)
                ins.then_inc(self.sem("masked"), 1)

    def tensor(self, pe):
        k = self.k
        def turn(bank, of, meta_bank):
            for n in range(self.PAIRS):
                ins = pe.transpose(k.ps[:, bank, n * P:(n + 1) * P], of[:, N_META + n * P:N_META + (n + 1) * P], k.ident[:])
            if meta_bank is not None:
                ins = pe.transpose(k.ps[0:N_META, meta_bank, 0:P], of[:, 0:N_META], k.ident[:])
            ins.then_inc(self.sem("turned"), 1)

        with pe.Fori(0, HYT) as i:
            self.wait(pe, "v", i + 1)
            turn(0, self.vT, 1)
            for d in range(2):
                self.wait(pe, "scaled", i * 2 + (d + 1))
                turn(2 + d, self.kd[d], 6 if d == 0 else None)
            for d in range(2):
                for n in range(self.PAIRS):
                    for row, part, first, end in self.quarters(d):
                        at = n * P + part * CH
                        ins = pe.matmul(k.ps[row:row + CH // 2, 4 + d, n * CH + first:n * CH + end], self.ks[d][:, n * P + row:n * P + row + CH // 2],
                                        self.qs[d][:, at + first:at + end], start=True, stop=True)
                ins.then_inc(self.sem("scored"), 1)
            for d in range(2):
                self.wait(pe, "tok", i * 3 + (3 if d == 0 else 3))
                for n in range(NCH - d):
                    if d == 0 and n == 0:
                        ins = pe.matmul(self.added(0, 0), self.kdtok[d][0:N_META, self.PAIRS], self.vtok[0:N_META, self.PAIRS], start=True, stop=True)
                    else:
                        c = self.ORDER[d][n - 1 if d == 0 else n]
                        rows = slice((c % 2) * CH, (c % 2 + 1) * CH)
                        ins = pe.matmul(self.added(d, n), self.kdtok[d][rows, c // 2], self.vtok[rows, c // 2], start=True, stop=True)
                ins.then_inc(self.sem("u"), 1)
            self.wait(pe, "masked", i * 2 + 2)
            self.wait(pe, "state", i * (2 * NCH - 3) + (2 * NCH - 3))
            for c in range(NCH):
                rows = slice((c % 2) * CH, (c % 2 + 1) * CH)
                at = slice(c * CH, (c + 1) * CH)
                terms = []
                for d in range(2):
                    terms.append((self.vtok[rows, c // 2], self.A[d][rows, c // 2]))
                    n = c if d == 0 else NCH - 2 - c
                    if n >= 0:
                        terms.append((self.S[d][:, n, :], self.qe[d][:, at]))
                for n, (lhsT, rhs) in enumerate(terms):
                    ins = pe.matmul(k.ps[:, (7, 5)[c % 2], at], lhsT, rhs, start=(n == 0), stop=(n == len(terms) - 1))
            ins.then_inc(self.sem("o"), 1)


class MixerOut:

    BANKS = 4

    def __init__(self, k, stream, source):
        self.k, self.stream, self.source = k, stream, source

    def sync(self, sp):
        self.stream.load_run(sp, [tiles_of(self.k.ins["w_out_2"])], KD, 2 * P, KD // 2)

    def tensor(self, pe, stream):
        k = self.k
        pe.sem_inc(k.sem("mixed"), self.BANKS)

        def chunk(n, i, c):
            stream.landed(pe, n, i)
            w = stream.slot(n, KD, 2 * P)
            for f in range(2):
                j = 2 * c + f
                pe.wait_ge(k.sem("mixed"), i * (2 * NSLOT) + (j + 1))
                for r in range(KD):
                    ins = pe.matmul(k.ps[:, j % self.BANKS, :], w[:, r, f * P:(f + 1) * P], self.source(r), start=(r == 0), stop=(r == KD - 1))
                stream.group_done(ins, f == 1)

        stream.rounds(pe, KD // 2, 2, chunk)

    def vector(self, dve, stream):
        k = self.k

        def chunk(n, i, c):
            for f in range(2):
                j = 2 * c + f
                stream.wait_group(dve, n, i, c, f)
                dve.tensor_tensor(k.xT[:, j, :], k.xT[:, j, :], k.ps[:, j % self.BANKS, :], ALU.add).then_inc(k.sem("mixed"), 1)

        stream.rounds(dve, KD // 2, 2, chunk)

    def scalar(self, act, stream):
        stream.skip(KD // 2, 2)

    def gpsimd(self, pool):
        pass



POS = [(n, min(P, L2 - n * P)) for n in range(FQT)]
FREQ = [(n, min(P, N_FREQ - n * P)) for n in range(FQT)]
HALVES = [slice(0, HALF), slice(HALF, L2)]
EMB = 33
HID = 64


class Hyena:

    def __init__(self, k, kept):
        self.k = k
        room = Room(k.arena[:, kept:])
        self.u = room.take(3 * HYT, L2)
        self.cos = room.take(FQT, N_FREQ)
        self.sin = room.take(FQT, N_FREQ)
        self.Pq = room.take(2, FQT, W_HY)
        self.EF = room.take(2, FQT, W_HY)
        self.z = room.take(FQT, W_HY)
        self.window = room.take(FQT, W_HY)
        self.small = room.take(FQT + 1)
        side = Room(k.hT[:].rearrange("p j t -> p (j t)"))
        self.w3 = side.take(4, W_HY)
        self.w3_now = side.take(2, W_HY)
        self.emb = self.Pq.rearrange("p a t c -> p (a t c)")[:, 0:L2]
        self.w1 = side.take(HID)
        self.w2 = side.take(HID)
        self.bias = side.take(3)
        self.hid = side.take(L2)
        self.turns = self.z.rearrange("p t c -> p (t c)")[:, 0:L2]
        self.tmp = room.take(2, W_HY)

    def sync(self, sp):
        k = self.k
        k.stage_over(sp, k.base + 6)
        k.load_tables(sp, "hyena", [
            (to, k.tables[name]) for to, name in ((self.cos, "t_cos"), (self.sin, "t_sin"))])

    def sync_filter(self, sp):
        k = self.k
        k.stage_over(sp, k.base + 7)
        col = lambda name: k.ins[name].rearrange("(h o) -> h o", o=1)
        k.load_tables(sp, "filter", [
            (self.window, k.tables["t_window"]), (self.small[:, 0:FQT], k.tables["t_wk"]), (self.small[:, FQT:], k.tables["t_not_first"]),
            (self.w3[0:HID], k.ins["filt_w3_2"].rearrange("h (n c) -> h n c", n=4)), (self.emb[0:EMB], k.tables["t_emb"]),
            (self.w1[0:EMB], k.ins["filt_w1_2"]), (self.w2[0:HID], k.ins["filt_w2_2"]), (self.bias[0:HID, 0:1], col("filt_b1_2")),
            (self.bias[0:HID, 1:2], col("filt_b2_2")), (self.bias[0:HID, 2:3], col("filt_freq_2"))])


    TURN = float(1.5 * 2 ** 23)
    PI2 = (6.28125, 0.0019353071795864769)

    def vector_front(self, dve, st):
        k = self.k
        with dve.Fori(0, 3 * HYT) as i:
            st.enter(i, 4)
            u = self.u[:, bass.ds(i, 1), :].rearrange("p o t -> p (o t)")
            w = lambda tap: k.col("conv_w_2", i + tap * 3 * HYT)
            conv = self.tmp.rearrange("p a b -> p (a b)")[:, 0:L2]
            st.done(dve.tensor_scalar(conv, u, w(1), k.col("conv_b_2", i + 0), ALU.mult, ALU.add))
            st.wait()
            st.done(dve.scalar_tensor_tensor(conv[:, 1:], u[:, 0:L2 - 1], w(0), conv[:, 1:], ALU.mult, ALU.add))
            st.wait()
            st.done(dve.scalar_tensor_tensor(conv[:, 0:L2 - 1], u[:, 1:], w(2), conv[:, 0:L2 - 1], ALU.mult, ALU.add))
            st.wait()
            st.done(dve.tensor_scalar(u, conv, 1.0, None, ALU.mult))
            st.wait()
            st.leave(3 * HYT)
        k.wait_tables(dve, "filter")
        x, turns = self.hid[0:HID], self.turns[0:HID]
        for layer in range(2):
            dve.wait_ge(k.sem("hy_net"), layer + 1)
            for n, half in enumerate(HALVES):
                ins = dve.tensor_scalar(x[:, half], k.ps[0:HID, n, 0:HALF], self.bias[0:HID, layer:layer + 1], self.bias[0:HID, 2:3], ALU.add, ALU.mult)
            st.done(ins)
            st.wait()
            st.done(dve.tensor_scalar(turns, x, 1.0 / (2 * np.pi), self.TURN, ALU.mult, ALU.add))
            st.wait()
            st.done(dve.tensor_scalar(turns, turns, self.TURN, None, ALU.subtract))
            for part in self.PI2:
                st.wait()
                st.done(dve.scalar_tensor_tensor(x, turns, -part, x, ALU.mult, ALU.add))
            st.wait()
            dve.tensor_scalar(x, x, float(np.float32(3.1415925)), -float(np.float32(3.1415925)), ALU.min, ALU.max).then_inc(k.sem("hy_angle"), 1)

    def scalar_front(self, act):
        k = self.k
        for layer in range(2):
            act.wait_ge(k.sem("hy_angle"), layer + 1)
            act.activation(self.hid[0:HID], self.hid[0:HID], ACT.Sin).then_inc(k.sem("hy_sine"), 1)

    def tensor_front(self, pe):
        k = self.k
        k.wait_tables(pe, "filter")
        for layer, (w, of) in enumerate(((self.w1[0:EMB], self.emb[0:EMB]), (self.w2[0:HID], self.hid[0:HID]))):
            if layer:
                pe.wait_ge(k.sem("hy_sine"), 1)
            for n, half in enumerate(HALVES):
                ins = pe.matmul(k.ps[0:HID, n, 0:HALF], w, of[:, half], start=True, stop=True)
            ins.then_inc(k.sem("hy_net"), 1)


    def tensor(self, pe):
        k = self.k
        mm = pe.matmul
        k.wait_tables(pe, "filter")
        with pe.Fori(0, 2) as i:
            pe.wait_ge(k.sem("hy_w3"), i + 1)
            for n, rows in POS:
                if 2 <= n < FQT - 1:
                    pe.wait_ge(k.sem("hy_filtered"), i * FQT + (n if n == FQT - 2 else n - 1))
                for d in range(2):
                    ins = mm(k.ps[0:rows, 2 * (n % 2) + d, :], self.hid[0:HID, n * P:n * P + rows], self.w3_now[0:HID, d], start=True, stop=True)
                ins.then_inc(k.sem("hy_filter"), 1)
            for n, rows in POS:
                if n >= 2:
                    pe.wait_ge(k.sem("hy_z"), i * FQT + (n - 1))
                for c in range(HYT):
                    ins = pe.transpose(k.ps[0:rows, 6 + n % 2, c * P:(c + 1) * P], self.u[:, c, n * P:n * P + rows], k.ident[:])
                ins.then_inc(k.sem("hy_turned"), 1)
            pe.wait_ge(k.sem("hy_filtered"), i * FQT + FQT)
            for n, rows in FREQ:
                if n >= 2:
                    pe.wait_ge(k.sem("hy_spectrum"), i * FQT + (n - 1))
                for d, table in enumerate((self.cos, self.sin)):
                    for t, depth in POS:
                        ins = mm(k.ps[0:rows, 2 * (n % 2) + d, :], table[0:depth, t, n * P:n * P + rows], self.EF[0:depth, d, t, :],
                                 start=(t == 0), stop=(t == FQT - 1))
                ins.then_inc(k.sem("hy_transformed"), 1)
            pe.wait_ge(k.sem("hy_z"), i * FQT + FQT)
            for n, rows in FREQ:
                if n >= 2:
                    pe.wait_ge(k.sem("hy_product"), i * FQT + (n - 1))
                for d, table in enumerate((self.cos, self.sin)):
                    for t, depth in POS:
                        ins = mm(k.ps[0:rows, 4 + 2 * (n % 2) + d, :], table[0:depth, t, n * P:n * P + rows], self.z[0:depth, t, :],
                                 start=(t == 0), stop=(t == FQT - 1))
                ins.then_inc(k.sem("hy_z_transformed"), 1)
            pe.wait_ge(k.sem("hy_product"), i * FQT + FQT)
            pe.wait_ge(k.sem("hy_spectrum"), i * FQT + FQT)
            for c in range(HYT):
                if c >= 2:
                    pe.wait_ge(k.sem("hy_gated"), i * HYT + (c - 1))
                for h, half in enumerate(HALVES):
                    for d, table in enumerate((self.cos, self.sin)):
                        for t, depth in FREQ:
                            ins = mm(k.ps[:, 2 * (c % 2) + h, 0:HALF], self.EF[0:depth, d, t, c * P:(c + 1) * P], table[0:depth, t, half],
                                     start=(d == 0 and t == 0), stop=(d == 1 and t == FQT - 1))
                ins.then_inc(k.sem("hy_inverted"), 1)
            pe.wait_ge(k.sem("hy_gated"), i * HYT + HYT)

    def vector(self, dve, st):
        k = self.k
        one = lambda ap: ap.rearrange("p o t -> p (o t)")
        with dve.Fori(0, 2) as i:
            st.enter(i, 2 * FQT + HYT)
            for n, rows in POS:
                dve.wait_ge(k.sem("hy_filter"), i * FQT + (n + 1))
                if n >= 1:
                    dve.wait_ge(k.sem("hy_filtered"), i * FQT + n)
                f, b = self.tmp[0:rows, 0], self.tmp[0:rows, 1]
                win = self.window[0:rows, n]
                dve.tensor_tensor(f, k.ps[0:rows, 2 * (n % 2), :], win, ALU.mult)
                keep = self.small[0:rows, FQT:FQT + 1] if n == 0 else 1.0
                st.done(dve.scalar_tensor_tensor(b, k.ps[0:rows, 2 * (n % 2) + 1, :], keep, win, ALU.mult, ALU.mult))
                st.wait()
                dve.tensor_tensor(self.EF[0:rows, 0, n, :], f, b, ALU.add)
                dve.tensor_tensor(self.EF[0:rows, 1, n, :], f, b, ALU.subtract).then_inc(k.sem("hy_filtered"), 1)
            for n, rows in FREQ:
                dve.wait_ge(k.sem("hy_z_transformed"), i * FQT + (n + 1))
                dve.wait_ge(k.sem("hy_spectrum"), i * FQT + FQT)
                a, b = k.ps[0:rows, 4 + 2 * (n % 2), :], k.ps[0:rows, 5 + 2 * (n % 2), :]
                p, q = self.Pq[0:rows, 0, n], self.Pq[0:rows, 1, n]
                e, f = self.EF[0:rows, 0, n], self.EF[0:rows, 1, n]
                dve.tensor_tensor(e, a, p, ALU.mult)
                dve.tensor_tensor(f, a, q, ALU.mult)
                dve.tensor_tensor(q, b, q, ALU.mult)
                st.done(dve.tensor_tensor(p, b, p, ALU.mult))
                st.wait()
                dve.tensor_tensor(e, e, q, ALU.subtract)
                dve.tensor_tensor(f, f, p, ALU.add).then_inc(k.sem("hy_product"), 1)
            for c in range(HYT):
                dve.wait_ge(k.sem("hy_inverted"), i * HYT + (c + 1))
                z = self.u[:, c, :].rearrange("p (h t) -> p h t", h=2)
                skip = k.col("filt_skip_2", i * HYT + c)
                st.done(dve.scalar_tensor_tensor(z, z, skip, k.ps[:, 2 * (c % 2):2 * (c % 2) + 2, 0:HALF], ALU.mult, ALU.add))
                st.wait()
                gate = one(self.u[:, bass.ds(i * HYT + (HYT + c), 1), :])
                dve.tensor_tensor(self.u[:, c, :], self.u[:, c, :], gate, ALU.mult).then_inc(k.sem("hy_gated"), 1)
            st.leave(2)

    def scalar(self, act):
        k = self.k
        with act.Fori(0, 2) as i:
            for n, rows in POS:
                act.wait_ge(k.sem("hy_turned"), i * FQT + (n + 1))
                act.activation(self.z[0:rows, n], k.ps[0:rows, 6 + n % 2, :], ACT.Copy).then_inc(k.sem("hy_z"), 1)
            for n, rows in FREQ:
                act.wait_ge(k.sem("hy_transformed"), i * FQT + (n + 1))
                for d in range(2):
                    ins = act.activation(self.Pq[0:rows, d, n], k.ps[0:rows, 2 * (n % 2) + d, :], ACT.Identity, scale=self.small[0:rows, n:n + 1])
                ins.then_inc(k.sem("hy_spectrum"), 1)

    def gpsimd(self, pool):
        k = self.k
        for order in range(2):
            if order:
                pool.wait_ge(k.sem("hy_filtered"), FQT)
            pool.tensor_copy(self.w3_now[0:HID], self.w3[0:HID, order::2, :]).then_inc(k.sem("hy_w3"), 1)



EXP_ROOM = 3 * 4 * D


class MoeRoom:

    def __init__(self, k):
        self.k = k
        early = Room(k.arena[:, 2 * HYT * L2:])
        self.w_router = early.take(KD, N_GROUPS + NE)
        self.strict = early.take(P)
        self.countdown = early.take(8)
        self.expert = early.take(NE)
        self.final_gain = early.take(D)
        self.weights_at = k.arena[:, ARENA_W - 2 * EXP_ROOM:]
        assert 2 * HYT * L2 + early.regions[0][1] <= ARENA_W - 2 * EXP_ROOM
        weights = Room(self.weights_at)
        self.w_gate = [weights.take(KD, D_EXP) for _ in range(2)]
        self.w_up = [weights.take(KD, D_EXP) for _ in range(2)]
        self.w_down = [weights.take(D_EXP // P, D) for _ in range(2)]
        late = Room(k.arena[:, 0:2 * HYT * L2], k.ring[:].rearrange("p s c -> p (s c)"))
        self.xeT = [late.take(KD, SLOTS) for _ in range(2)]
        self.silu = [late.take(D_EXP)[0:SLOTS] for _ in range(2)]
        self.act = [late.take(D_EXP)[0:SLOTS] for _ in range(2)]
        self.actT = [late.take(D_EXP // P, SLOTS) for _ in range(2)]
        self.hn = late.take(TT, D)
        self.xe = [late.take(D)[0:SLOTS] for _ in range(2)]
        self.y = [late.take(D)[0:SLOTS] for _ in range(2)]
        self.gates = late.take(2, TT)
        self.late = late
        self.slot = k.sb("slot", [P, 2 * TT], U32)
        self.over_expert = k.sb("over_expert", [1, OVER + 1], I32)


class Router:

    def __init__(self, k, m):
        self.k, self.m = k, m
        room = m.late
        self.logits = room.take(TT, N_GROUPS + NE)
        self.small = room.take(8, TT, 8)
        self.one = room.take(10, TT)
        self.wide = room.take(4, TT * NE)
        self.rows = room.take(4, NE)

    def sync(self, sp):
        k, m = self.k, self.m
        k.stage_over(sp, k.base + 9)
        k.load_tables(sp, "router", [
            (m.w_router[:, :, 0:N_GROUPS], tiles_of(k.ins["w_router_group_2"])),
            (m.w_router[:, :, N_GROUPS:], k.ins["w_router_expert_2"].rearrange("(k p) g e -> p k (g e)", p=P)),
            (m.strict, k.tables["t_strict"]), (m.countdown, k.tables["t_countdown"]), (m.expert, k.tables["t_expert"]),
            (m.final_gain, k.ins["norm_final_2"].rearrange("(o d) -> o d", o=1).to_broadcast([P, D]))])

    def tensor(self, pe):
        k, m = self.k, self.m
        k.wait_tables(pe, "router")
        for t in range(TT):
            for r in range(KD):
                ins = pe.matmul(k.ps[:, t, 0:N_GROUPS + NE], k.hT[:, r, t * P:(t + 1) * P], m.w_router[:, r, :], start=(r == 0), stop=(r == KD - 1))
            ins.then_inc(k.sem("router_logits"), 1)
        for t in range(TT):
            if t >= 2:
                pe.wait_ge(k.sem("hn_copied"), t - 1)
            for r in range(KD):
                ins = pe.transpose(k.ps[:, 4 + 2 * (t % 2) + r // 4, r % 4 * P:(r % 4 + 1) * P], k.hT[:, r, t * P:(t + 1) * P], k.ident[:])
            ins.then_inc(k.sem("hn_turned"), 1)
        pe.wait_ge(k.sem("router_chosen"), 1)
        chosen = self.wide[:, 2, :].rearrange("p (t e) -> p t e", t=TT)
        for t in range(TT):
            for s in range(t + 1):
                ins = pe.matmul(k.ps[:, 0, t * NE:(t + 1) * NE], k.ones[:] if s < t else m.strict, chosen[:, s, :], start=(s == 0), stop=(s == t))
        for t in range(TT):
            ins = pe.matmul(k.ps[:, 1, 0:NE], k.ones[:], chosen[:, t, :], start=(t == 0), stop=(t == TT - 1))
        ins.then_inc(k.sem("router_counted"), 1)

    def scalar(self, act):
        k, m = self.k, self.m
        for t in range(TT):
            act.wait_ge(k.sem("hn_turned"), t + 1)
            act.activation(m.hn[:, t, :].rearrange("p (b c) -> p b c", b=2), k.ps[:, 4 + 2 * (t % 2):6 + 2 * (t % 2), :], ACT.Copy).then_inc(k.sem("hn_copied"), 1)
        act.wait_ge(k.sem("router_diff"), 1)
        act.activation(self.small[:, 1], self.small[:, 1], ACT.Exp).then_inc(k.sem("router_exp"), 1)
        act.wait_ge(k.sem("router_diff"), 2)
        act.activation(self.one[:, 5, :], self.one[:, 4, :], ACT.Exp).then_inc(k.sem("router_exp"), 1)

    def vector(self, dve, st):
        k, m = self.k, self.m

        def do(ins):
            st.done(ins)
            st.wait()

        col = lambda n: self.one[:, n, :].unsqueeze(2)
        spread = lambda ap, n: ap.to_broadcast([P, TT, n])
        each = lambda row, n: row.unsqueeze(1).to_broadcast([P, TT, n])
        for t in range(TT):
            dve.wait_ge(k.sem("router_logits"), t + 1)
            ins = dve.tensor_copy(self.logits[:, t, :], k.ps[:, t, 0:N_GROUPS + NE])
        do(ins)
        groups = self.logits[:, :, 0:N_GROUPS]
        experts = self.logits[:, :, N_GROUPS:].rearrange("p t (g e) -> p t e g", g=N_GROUPS)
        tmp, e_group, of_group, e_logits, first, second = (self.small[:, n] for n in range(6))

        def first_largest(out, x, largest):
            do(dve.tensor_reduce(largest, x, AX.X, ALU.max))
            do(dve.tensor_tensor(tmp, x, spread(largest, 8), ALU.is_equal))
            do(dve.tensor_tensor(tmp, tmp, each(m.countdown, 8), ALU.mult))
            do(dve.tensor_reduce(col(9), tmp, AX.X, ALU.max))
            do(dve.tensor_tensor(out, tmp, spread(col(9), 8), ALU.is_equal))

        first_largest(of_group, groups, col(0))
        dve.tensor_tensor(e_group, groups, spread(col(0), 8), ALU.subtract).then_inc(k.sem("router_diff"), 1)
        by_group = self.wide[:, 3, :].rearrange("p (t e g) -> p t e g", t=TT, g=N_GROUPS)
        for t in range(TT):
            ins = dve.tensor_tensor(by_group[:, t], experts[:, t], of_group[:, t].unsqueeze(1).to_broadcast([P, PER_GROUP, N_GROUPS]), ALU.mult)
        do(ins)
        do(dve.tensor_reduce(e_logits.unsqueeze(3), by_group, AX.X, ALU.add))
        first_largest(first, e_logits, col(1))
        do(dve.scalar_tensor_tensor(e_logits, first, -1e30, e_logits, ALU.mult, ALU.add))
        first_largest(second, e_logits, col(2))
        dve.tensor_tensor(self.one[:, 4, :], self.one[:, 2, :], self.one[:, 1, :], ALU.subtract).then_inc(k.sem("router_diff"), 1)
        wide = lambda n: self.wide[:, n, :].rearrange("p (t g e) -> p t g e", t=TT, g=N_GROUPS)
        for n, choice in enumerate((first, second)):
            for t in range(TT):
                ins = dve.tensor_tensor(wide(n)[:, t], of_group[:, t].unsqueeze(2).to_broadcast([P, N_GROUPS, PER_GROUP]),
                                        choice[:, t].unsqueeze(1).to_broadcast([P, N_GROUPS, PER_GROUP]), ALU.mult)
        do(ins)
        dve.tensor_tensor(self.wide[:, 2, :], self.wide[:, 0, :], self.wide[:, 1, :], ALU.add).then_inc(k.sem("router_chosen"), 1)
        dve.wait_ge(k.sem("router_exp"), 2)
        do(dve.tensor_reduce(col(3), e_group, AX.X, ALU.add))
        do(dve.scalar_tensor_tensor(self.one[:, 6, :], self.one[:, 5, :], 1.0, self.one[:, 3, :], ALU.add, ALU.mult))
        do(dve.reciprocal(m.gates[:, 0, :], self.one[:, 6, :]))
        dve.tensor_tensor(m.gates[:, 1, :], m.gates[:, 0, :], self.one[:, 5, :], ALU.mult)
        dve.wait_ge(k.sem("router_counted"), 1)
        count, more, upto, base = (self.rows[:, n, :] for n in range(4))
        do(dve.tensor_copy(count, k.ps[:, 1, 0:NE]))
        do(dve.tensor_scalar(more, count, float(SLOTS), None, ALU.is_gt))
        for n in range(2, T // SLOTS):
            do(dve.scalar_tensor_tensor(more, count, float(n * SLOTS), more, ALU.is_gt, ALU.add))
        do(dve.memset(base, 1.0))
        do(dve.tensor_tensor_scan(upto, base, more, 0.0, ALU.mult, ALU.add))
        do(dve.tensor_tensor(base, upto, more, ALU.subtract))
        do(dve.scalar_tensor_tensor(base, base, float(NE - 1), m.expert, ALU.add, ALU.subtract))
        order = self.wide[:, 3, :].rearrange("p (t e) -> p t e", t=TT)
        place = self.wide[:, 2, :].rearrange("p (t e) -> p t e", t=TT)
        do(dve.tensor_copy(self.wide[:, 3, :], k.ps[:, 0, 0:TT * NE]))
        do(dve.scalar_tensor_tensor(place, order, float(SLOTS), each(base, NE), ALU.is_ge, ALU.mult))
        do(dve.tensor_tensor(place, place, each(m.expert, NE), ALU.add))
        do(dve.scalar_tensor_tensor(place, place, float(SLOTS), order, ALU.mult, ALU.add))
        for n in range(2):
            do(dve.tensor_tensor(self.wide[:, n, :], self.wide[:, n, :], self.wide[:, 2, :], ALU.mult))
            do(dve.tensor_reduce(col(7 + n), self.wide[:, n, :].rearrange("p (t e) -> p t e", t=TT), AX.X, ALU.add))
            dve.tensor_copy(m.slot[:, n * TT:(n + 1) * TT], self.one[:, 7 + n, :]).then_inc(k.sem("slots_ready"), 1)
        found = self.small.rearrange("p a t e -> p (a t e)")[0:1, 0:OVER]
        for n in range(OVER):
            do(dve.tensor_scalar(base[0:1, :], upto[0:1, :], float(n), None, ALU.is_le))
            do(dve.tensor_reduce(found[:, n:n + 1], base[0:1, :], AX.X, ALU.add))
        do(dve.tensor_scalar(found, found, float(NE - 1), None, ALU.min))
        dve.tensor_copy(m.over_expert[:, 0:OVER], found)
        dve.tensor_copy(m.over_expert[:, OVER:], upto[0:1, NE - 1:NE])

    def gpsimd(self, pool):
        k, m = self.k, self.m
        pool.wait_ge(k.sem("slots_zeroed"), 16 * k.zero_writes)
        pool.wait_ge(k.sem("hn_copied"), TT)
        for n in range(2):
            pool.wait_ge(k.sem("slots_ready"), n + 1)
            for t in range(TT):
                at = n * TT + t
                pool.indirect_dma_start(k.x_slots, bass.IndirectOffsetOnAxis(ap=m.slot[:, at:at + 1], axis=0), m.hn[:, t, :], None).then_inc(k.sem("scattered"), 16)
        pool.wait_ge(k.sem("scattered"), 16 * 2 * TT)


def zero_slots(k, pool):
    blocks = lambda of: of.rearrange("(b s) d -> s b d", s=SLOTS)
    k.zero_writes = 0
    for to, first, end in ((k.x_slots, 0, NE // 2), (k.x_slots, NE // 2, NE), (k.x_slots, NE, NE + OVER), (k.y_slots, NE, NE + OVER)):
        pool.dma_start(blocks(to)[:, first:end, :], k.spare[0:SLOTS].unsqueeze(1).to_broadcast([SLOTS, end - first, D])).then_inc(k.sem("slots_zeroed"), 16)
        k.zero_writes += 1



HALF_D = [slice(0, D // 2), slice(D // 2, D)]


class Experts(Signals):

    def __init__(self, k, m):
        super().__init__(k, "moe", **{w: NE for w in ("x_turned", "x_copied", "act_turned")}, **{w: NE + 2 for w in ("gate", "up", "down", "silu", "acted")},
                         act_copied=NE + 1, y_copied=NE + 1, gate_in0=8 * NE, x_in0=8 * NE, y_out0=16 + 8 * NE)
        self.m = m

    def steps(self, eng, step):
        step(0, 0, False, True)
        step(0, 1, True, True)
        with eng.Fori(1, NE // 2 - 1) as i:
            for u in range(2):
                step(i, u, True, True)
        step(NE // 2 - 1, 0, True, True)
        step(NE // 2 - 1, 1, True, False)

    def sync(self, sp):
        k, m = self.k, self.m
        for what in ("gate", "up", "down"):
            sp.sem_inc(self.sem(what), 2)
        block = lambda of, e: of[bass.ds(e * SLOTS, SLOTS), :]

        def load_w(i, u, what, to, src):
            self.wait(sp, what, i * 2 + (u + 1))
            of = k.ins[src][bass.ds(i * 2 + u, 1)].rearrange("o (k p) n -> p (o k) n", p=P)
            sp.dma_start(to[u], of).then_inc(self.sem(f"{what}_in{u}"), 16)

        def load_x(e, u):
            sp.dma_start(m.xe[u], block(k.x_slots, e)).then_inc(self.sem(f"x_in{u}"), 16)

        def store_y(e, u):
            self.wait(sp, "y_copied", e + 2)
            sp.dma_start(block(k.y_slots, e), m.y[u]).then_inc(self.sem(f"y_out{u}"), 16)

        def step(i, u, next):
            load_w(i, u, "gate", m.w_gate, "w_gate_2")
            load_w(i, u, "up", m.w_up, "w_up_2")
            if next:
                self.wait(sp, "x_turned", i * 2 + u)
                load_x(i * 2 + (u + 1), 1 - u)
            load_w(i, u, "down", m.w_down, "w_down_2")
            store_y(i * 2 + (u - 2), u)

        for u in range(2):
            load_w(0, u, "gate", m.w_gate, "w_gate_2")
            load_w(0, u, "up", m.w_up, "w_up_2")
            load_w(0, u, "down", m.w_down, "w_down_2")
        sp.wait_ge(k.sem("scattered"), 16 * 2 * TT)
        for u in range(2):
            load_x(u, u)
        self.wait(sp, "x_turned", 1)
        load_x(2, 0)
        with sp.Fori(1, NE // 2 - 1) as i:
            for u in range(2):
                step(i, u, True)
        step(NE // 2 - 1, 0, True)
        step(NE // 2 - 1, 1, False)
        for u in range(2):
            store_y(NE - 2 + u, u)
        for u in range(2):
            self.wait(sp, f"y_out{u}", 16 + 16 * (NE // 2))

    def tensor(self, pe):
        k, m = self.k, self.m
        pe.sem_inc(self.sem("silu"), 2)
        pe.sem_inc(self.sem("acted"), 2)
        pe.sem_inc(self.sem("act_copied"), 1)
        pe.sem_inc(self.sem("y_copied"), 1)

        def turn_x(u):
            for r in range(KD):
                ins = pe.transpose(k.ps[:, 0, r * SLOTS:(r + 1) * SLOTS], m.xe[u][:, r * P:(r + 1) * P], k.ident[0:SLOTS, 0:SLOTS])
            ins.then_inc(self.sem("x_turned"), 1)

        def x_landed(i, u):
            self.wait(pe, f"x_in{u}", i * 16 + 16)

        def project(w, u, bank, done, ahead):
            for r in range(KD):
                if r == KD - 1:
                    ahead()
                ins = pe.matmul(k.ps[0:SLOTS, bank, :], m.xeT[u][:, r, :], w[u][:, r, :], start=(r == 0), stop=(r == KD - 1))
            ins.then_inc(self.sem(done), 1)

        def act_ready(e):
            self.wait(pe, "acted", e + 2)
            self.wait(pe, "act_copied", e)

        def turn_act(u):
            for r in range(D_EXP // P):
                ins = pe.transpose(k.ps[:, 1, r * SLOTS:(r + 1) * SLOTS], m.act[u][:, r * P:(r + 1) * P], k.ident[0:SLOTS, 0:SLOTS])
            ins.then_inc(self.sem("act_turned"), 1)

        def down(e, u, i):
            self.wait(pe, f"down_in{u}", i * 16)
            self.wait(pe, "act_copied", e + 1)
            self.wait(pe, "y_copied", e)
            for h, half in enumerate(HALF_D):
                for r in range(D_EXP // P):
                    ins = pe.matmul(k.ps[0:SLOTS, 6 + h, :], m.actT[u][:, r, :], m.w_down[u][:, r, half], start=(r == 0), stop=(r == D_EXP // P - 1))
            ins.then_inc(self.sem("down"), 1)

        def step(i, u, prev, next):
            e = i * 2 + u
            self.wait(pe, "x_copied", e + 1)
            self.wait(pe, f"gate_in{u}", i * 16 + 16)
            self.wait(pe, "silu", e + 1)
            project(m.w_gate, u, 2 + u, "gate", lambda: act_ready(e) if prev else None)
            if prev:
                turn_act(1 - u)
            self.wait(pe, f"up_in{u}", i * 16 + 16)
            self.wait(pe, "acted", e + 1)
            project(m.w_up, u, 4 + u, "up", lambda: x_landed(i + u, 1 - u) if next else None)
            if next:
                turn_x(1 - u)
            if prev:
                down(e, 1 - u, i + u)

        x_landed(0, 0)
        turn_x(0)
        self.steps(pe, step)
        act_ready(NE)
        turn_act(1)
        down(NE, 1, NE // 2)

    def scalar(self, act):
        k, m = self.k, self.m
        for u in range(2):
            act.sem_inc(self.sem(f"y_out{u}"), 16)

        def copy_y(e, u, i):
            self.wait(act, "down", e + 2)
            self.wait(act, f"y_out{u}", i * 16)
            act.activation(m.y[u].rearrange("p (h c) -> p h c", h=2), k.ps[0:SLOTS, 6:8, :], ACT.Copy).then_inc(self.sem("y_copied"), 1)

        def step(i, u, prev, next):
            e = i * 2 + u
            self.wait(act, "gate", e + 3)
            self.wait(act, "acted", e + 1)
            act.activation(m.silu[u], k.ps[0:SLOTS, 2 + u, :], ACT.Silu).then_inc(self.sem("silu"), 1)
            if prev:
                copy_y(e, 1 - u, i + u)

        self.steps(act, step)
        copy_y(NE, 1, NE // 2)

    def vector(self, dve):
        k, m = self.k, self.m

        def copy_x(e, u):
            self.wait(dve, "x_turned", e + 1)
            dve.tensor_scalar(m.xeT[u].rearrange("p r s -> p (r s)"), k.ps[:, 0, 0:KD * SLOTS], 1.0, None, ALU.mult).then_inc(self.sem("x_copied"), 1)

        def copy_act(e, u):
            self.wait(dve, "act_turned", e)
            dve.tensor_scalar(m.actT[u].rearrange("p r s -> p (r s)"), k.ps[:, 1, 0:D_EXP // P * SLOTS], 1.0, None, ALU.mult).then_inc(self.sem("act_copied"), 1)

        def step(i, u, prev, next):
            e = i * 2 + u
            if prev:
                copy_act(e, 1 - u)
            self.wait(dve, "up", e + 3)
            self.wait(dve, "silu", e + 3)
            dve.tensor_tensor(m.act[u], m.silu[u], k.ps[0:SLOTS, 4 + u, :], ALU.mult).then_inc(self.sem("acted"), 1)
            if next:
                copy_x(e + 1, 1 - u)

        copy_x(0, 0)
        self.steps(dve, step)
        copy_act(NE, 1)

    def gpsimd(self, pool):
        for u in range(2):
            self.wait(pool, f"y_out{u}", 16 + 16 * (NE // 2))


class FurtherBlocks(Signals):

    def __init__(self, k, m):
        super().__init__(k, "moe", **{w: 0 for w in ("x_turned", "x_copied", "act_turned", "up", "down", "silu", "acted", "act_copied", "y_copied",
                                               "gate_in0", "x_in0", "y_out0")})
        self.m = m

    def any(self, eng):
        n = eng.value_load(self.m.over_expert[0:1, OVER:OVER + 1], min_val=0, max_val=OVER)
        return eng.If(n > 0)

    def sync(self, sp):
        k, m = self.k, self.m
        block = lambda of, j: of[(NE + j) * SLOTS:(NE + j + 1) * SLOTS, :]
        k.stage_over(sp, k.base + 14)
        with self.any(sp):
            for j in range(OVER):
                e = sp.value_load(m.over_expert[0:1, j:j + 1], min_val=0, max_val=NE - 1)
                if j:
                    self.wait(sp, "down", j)
                for to, src in ((m.w_gate, "w_gate_2"), (m.w_up, "w_up_2"), (m.w_down, "w_down_2")):
                    sp.dma_start(to[0], k.ins[src][bass.ds(e, 1)].rearrange("o (k p) n -> p (o k) n", p=P)).then_inc(self.sem("gate_in0"), 16)
                sp.dma_start(m.xe[0], block(k.x_slots, j)).then_inc(self.sem("x_in0"), 16)
                self.wait(sp, "y_copied", j + 1)
                sp.dma_start(block(k.y_slots, j), m.y[0]).then_inc(self.sem("y_out0"), 16)
            self.wait(sp, "y_out0", 16 + 16 * OVER)

    def tensor(self, pe):
        k, m = self.k, self.m
        small = k.ident[0:SLOTS, 0:SLOTS]
        with self.any(pe):
            with pe.Fori(0, OVER) as j:
                self.wait(pe, "x_in0", j * 16 + 16)
                for r in range(KD):
                    ins = pe.matmul(k.ps[:, 0, r * SLOTS:(r + 1) * SLOTS], m.xe[0][:, r * P:(r + 1) * P], small, start=True, stop=True)
                ins.then_inc(self.sem("x_turned"), 1)
                self.wait(pe, "x_copied", j + 1)
                self.wait(pe, "gate_in0", j * 48 + 48)
                for w, bank in ((m.w_gate, 2), (m.w_up, 4)):
                    for r in range(KD):
                        ins = pe.matmul(k.ps[0:SLOTS, bank, :], m.xeT[0][:, r, :], w[0][:, r, :], start=(r == 0), stop=(r == KD - 1))
                    ins.then_inc(self.sem("up"), 1)
                self.wait(pe, "acted", j + 1)
                for r in range(D_EXP // P):
                    ins = pe.matmul(k.ps[:, 1, r * SLOTS:(r + 1) * SLOTS], m.act[0][:, r * P:(r + 1) * P], small, start=True, stop=True)
                ins.then_inc(self.sem("act_turned"), 1)
                self.wait(pe, "act_copied", j + 1)
                for h, half in enumerate(HALF_D):
                    for r in range(D_EXP // P):
                        ins = pe.matmul(k.ps[0:SLOTS, 6 + h, :], m.actT[0][:, r, :], m.w_down[0][:, r, half], start=(r == 0), stop=(r == D_EXP // P - 1))
                ins.then_inc(self.sem("down"), 1)

    def scalar(self, act):
        k, m = self.k, self.m
        with self.any(act):
            act.sem_inc(self.sem("y_out0"), 16)
            with act.Fori(0, OVER) as j:
                self.wait(act, "up", j * 2 + 1)
                act.activation(m.silu[0], k.ps[0:SLOTS, 2, :], ACT.Silu).then_inc(self.sem("silu"), 1)
                self.wait(act, "down", j + 1)
                self.wait(act, "y_out0", j * 16 + 16)
                act.activation(m.y[0].rearrange("p (h c) -> p h c", h=2), k.ps[0:SLOTS, 6:8, :], ACT.Copy).then_inc(self.sem("y_copied"), 1)

    def vector(self, dve):
        k, m = self.k, self.m
        flat = lambda ap: ap.rearrange("p r s -> p (r s)")
        with self.any(dve):
            with dve.Fori(0, OVER) as j:
                self.wait(dve, "x_turned", j + 1)
                dve.tensor_scalar(flat(m.xeT[0]), k.ps[:, 0, 0:KD * SLOTS], 1.0, None, ALU.mult).then_inc(self.sem("x_copied"), 1)
                self.wait(dve, "up", j * 2 + 2)
                self.wait(dve, "silu", j + 1)
                dve.tensor_tensor(m.act[0], m.silu[0], k.ps[0:SLOTS, 4, :], ALU.mult).then_inc(self.sem("acted"), 1)
                self.wait(dve, "act_turned", j + 1)
                dve.tensor_scalar(flat(m.actT[0]), k.ps[:, 1, 0:D_EXP // P * SLOTS], 1.0, None, ALU.mult).then_inc(self.sem("act_copied"), 1)

    def gpsimd(self, pool):
        with self.any(pool):
            self.wait(pool, "y_out0", 16 + 16 * OVER)


class Combine:

    def __init__(self, k, m):
        self.k, self.m = k, m
        room = Room(m.weights_at)
        self.y = room.take(2, TT, D)
        self.sum = room.take(TT, D)
        self.square = room.take(D)
        self.total = room.take(TT)
        self.root = room.take(TT)

    def gpsimd(self, pool):
        k, m = self.k, self.m
        for t in range(TT):
            for n in range(2):
                at = n * TT + t
                pool.indirect_dma_start(self.y[:, n, t, :], None, k.y_slots, bass.IndirectOffsetOnAxis(ap=m.slot[:, at:at + 1], axis=0))\
                    .then_inc(k.sem(f"gathered{t // 2}"), 16)

    def tensor(self, pe):
        k = self.k
        for t in range(TT):
            if t >= 2:
                pe.wait_ge(k.sem("combined"), t - 1)
            for r in range(KD):
                ins = pe.transpose(k.ps[:, 2 * (t % 2) + r // 4, r % 4 * P:(r % 4 + 1) * P], k.xT[:, r, t * P:(t + 1) * P], k.ident[:])
            ins.then_inc(k.sem("h_turned"), 1)

    def vector(self, dve, st):
        k, m = self.k, self.m
        halves = lambda ap: ap.rearrange("p (b c) -> p b c", b=2)
        for t in range(TT):
            dve.wait_ge(k.sem("h_turned"), t + 1)
            dve.wait_ge(k.sem(f"gathered{t // 2}"), 64)
            gate = lambda n: m.gates[:, n, t:t + 1]
            dve.scalar_tensor_tensor(halves(self.sum[:, t]), halves(self.y[:, 0, t]), gate(0), k.ps[:, 2 * (t % 2):2 * (t % 2) + 2, :], ALU.mult, ALU.add)\
               .then_inc(k.sem("combined"), 1)
            dve.wait_ge(k.sem("combined"), t + 1)
            dve.scalar_tensor_tensor(self.sum[:, t], self.y[:, 1, t], gate(1), self.sum[:, t], ALU.mult, ALU.add).then_inc(k.sem("summed"), 1)
        for t in range(TT):
            dve.wait_ge(k.sem("final_root"), t + 1)
            st.done(dve.reciprocal(self.root[:, t:t + 1], self.root[:, t:t + 1]))
            st.wait()
            dve.scalar_tensor_tensor(self.sum[:, t], self.sum[:, t], self.root[:, t:t + 1], m.final_gain, ALU.mult, ALU.mult).then_inc(k.sem("final"), 1)

    def scalar(self, act):
        k = self.k
        for t in range(TT):
            act.wait_ge(k.sem("summed"), t + 1)
            act.activation(self.square, self.sum[:, t], ACT.Square, accum_out=self.total[:, t:t + 1]).then_inc(k.sem("final_square"), 1)
            act.wait_ge(k.sem("final_square"), t + 1)
            act.activation(self.root[:, t:t + 1], self.total[:, t:t + 1], ACT.Sqrt, bias=k.eps[:, 1:2], scale=1.0 / D).then_inc(k.sem("final_root"), 1)

    def sync(self, sp):
        k = self.k
        for t in range(TT):
            sp.wait_ge(k.sem("final"), t + 1)
            sp.dma_start(k.out[t * P:(t + 1) * P, :], self.sum[:, t]).then_inc(k.sem("out"), 16)
        sp.wait_ge(k.sem("out"), 16 * TT)


def block2(k, ins, st_sp):
    flat = lambda ap: ap.rearrange("p o t -> p (o t)")
    aligned = lambda ap: Room(ap[:, -ap.offset % 8:])
    mix_norm = FeatureNorm(k, Room(k.arena[:, 26000:]), KD, lambda j: k.hT[:, j, :], lambda j: k.hT[:, j, :], lambda j: k.col("norm_mix_2", j), HALVES)
    gates = HgrnGates(k)
    prepend = Prepend(k, gates)
    mix_input = SplitInput(k, KD, lambda r: k.hT[:, r, :], gates.input_room, L2)
    hgrn_in = MixerIn(k, st_sp, gates.tiles, 3 * W_HY, 5 * HYT // 2, Room(gates.rest), mix_input, True)
    hgrn = HgrnHeads(k, gates)

    def gated(dve, i, u, inv, norm):
        q, g = hgrn.tile(u, i * 2)[:, 0:T], hgrn.tile(4 * HYT + u, i * 2)[:, N_META:]
        dve.tensor_tensor(q, q, inv, ALU.mult).then_inc(norm.sem("inverted"), 1)
        norm.wait(dve, "inverted", i * 2 + (u + 3))
        dve.scalar_tensor_tensor(q, q, k.col("hgrn_norm_2", i * 2 + u), g, ALU.mult, ALU.mult)
    hgrn_norm = TileNorm(k, Room(gates.rest), HYT // 2, lambda i, u: hgrn.tile(u, i * 2)[:, 0:T], 1.0 / P, gated)
    hyena = Hyena(k, HYT * L2)
    hyena_in = MixerIn(k, st_sp, hyena.u, 0, 3 * HYT // 2, aligned(hyena.EF.rearrange("p a t c -> p (a t c)")), mix_input, False)
    z = lambda j: hyena.u[:, j, N_META:]
    hyena_norm = FeatureNorm(k, Room(k.hT[:].rearrange("p j t -> p (j t)")), HYT, z, z, lambda j: k.col("hyena_norm_2", j), [slice(0, T)])
    mix_out = MixerOut(k, st_sp, lambda r: z(r) if r < HYT else gates.tiles[:, r - HYT, 0:T])
    m = MoeRoom(k)
    ffn_norm = FeatureNorm(k, Room(k.ring[:].rearrange("p s c -> p (s c)")), KD, lambda j: k.xT[:, j, :], lambda j: k.hT[:, j, 0:T], lambda j: k.col("norm_ffn_2", j), [slice(0, T)])
    return prepend, mix_norm, hgrn_in, gates, hgrn, hgrn_norm, hyena_in, hyena, hyena_norm, mix_out, ffn_norm, Router(k, m), Experts(k, m), FurtherBlocks(k, m), Combine(k, m)



def program(nc, ins, tables, out, x_slots, y_slots):
    with ExitStack() as ctx:
        k = Core(nc, ctx, ins, tables, out, x_slots, y_slots)
        setup = Setup(k)
        cond = Conditioning(k)
        st_sp = Stream(k)
        din = DeltaIn(k, st_sp)
        room = lambda: Room(din.rest[:, din.free_at:])
        flat = lambda ap: ap.rearrange("p o t -> p (o t)")

        def unit(dve, i, u, inv, norm):
            x = flat(din.tiles[:, bass.ds(i + u * GH, 1), :])
            dve.scalar_tensor_tensor(x, x, (P ** -0.5, 1.0)[u], inv, ALU.mult, ALU.mult).then_inc(norm.sem("inverted"), 1)
        qk_norm = TileNorm(k, room(), GH, lambda i, u: flat(din.tiles[:, bass.ds(i + u * GH, 1), :]), 1.0, unit)
        heads = DeltaHeads(k, din)

        def gated(dve, i, u, inv, norm):
            at = lambda kind: flat(din.tiles[:, bass.ds(i * 2 + (u + kind * GH), 1), :])
            dve.tensor_tensor(at(0), at(0), inv, ALU.mult).then_inc(norm.sem("inverted"), 1)
            norm.wait(dve, "inverted", i * 2 + (u + 3))
            dve.scalar_tensor_tensor(at(0), at(0), k.col("gdn_norm_w", 0), at(3), ALU.mult, ALU.mult)
        o_norm = TileNorm(k, room(), GH // 2, lambda i, u: flat(din.tiles[:, bass.ds(i * 2 + u, 1), :]), 1.0 / P, gated)
        res0 = ResidualNorm(k, st_sp, tiles_of(ins["gdn_w_out"]), GH, 2, lambda r: din.tiles[:, r, :], room(), 0, 2, 0, (0, 3))
        up0 = FeedForwardUp(k, st_sp, 0)
        down0 = ResidualNorm(k, st_sp, tiles_of(ins["ffn_down"][0]), FT, 1, lambda r: up0.acts[:, r, :], up0.room, 0, 5, 1, (1, 0))
        rin = RetentionIn(k, st_sp)
        reth = RetentionHeads(k, rin)
        res1 = ResidualNorm(k, st_sp, tiles_of(ins["ret_w_out"]), 2 * KD, 1, lambda r: rin.gate[:, r, :], Room(rin.rest, k.arena[:, 0:2 * KD * T + TT * RH * R_DV]), 1, 2, 0, (1, 3))
        up1 = FeedForwardUp(k, st_sp, 1)
        down1 = ResidualNorm(k, st_sp, tiles_of(ins["ffn_down"][1]), FT, 1, lambda r: up1.acts[:, r, :], up1.room, 1, 5, 1, None)

        prepend, mix_norm, hgrn_in, gates, hgrn, hgrn_norm, hyena_in, hyena, hyena_norm, mix_out, ffn_norm, router, experts, further, combine = block2(k, ins, st_sp)

        block = ctx.enter_context(nc.Block())

        @block.sync
        def _(sp):
            setup.sync(sp)
            cond.sync(sp)
            din.sync(sp)
            res0.sync(sp)
            up0.sync(sp)
            down0.sync(sp)
            rin.sync(sp)
            reth.sync(sp)
            res1.sync(sp)
            up1.sync(sp)
            down1.sync(sp)
            prepend.sync(sp)
            hgrn_in.sync(sp)
            hyena_in.sync(sp)
            hyena.sync(sp)
            hyena.sync_filter(sp)
            mix_out.sync(sp)
            router.sync(sp)
            experts.sync(sp)
            further.sync(sp)
            combine.sync(sp)

        @block.tensor
        def _(pe):
            stream = Stream(k)
            setup.tensor(pe); k.meet(pe, "tensor")
            cond.tensor(pe); k.meet(pe, "tensor")
            din.tensor(pe, stream); k.meet(pe, "tensor")
            qk_norm.tensor(pe); k.meet(pe, "tensor")
            heads.tensor(pe); k.meet(pe, "tensor")
            o_norm.tensor(pe); k.meet(pe, "tensor")
            res0.tensor(pe, stream); k.meet(pe, "tensor")
            up0.tensor(pe, stream); k.meet(pe, "tensor")
            down0.tensor(pe, stream); k.meet(pe, "tensor")
            rin.tensor(pe, stream); k.meet(pe, "tensor")
            reth.tensor(pe); k.meet(pe, "tensor")
            res1.tensor(pe, stream); k.meet(pe, "tensor")
            up1.tensor(pe, stream); k.meet(pe, "tensor")
            down1.tensor(pe, stream); k.meet(pe, "tensor")
            prepend.tensor(pe); k.meet(pe, "tensor")
            mix_norm.tensor(pe); k.meet(pe, "tensor")
            hgrn_in.tensor(pe, stream); k.meet(pe, "tensor")
            gates.tensor(pe); k.meet(pe, "tensor")
            hgrn.tensor(pe); k.meet(pe, "tensor")
            hgrn_norm.tensor(pe); k.meet(pe, "tensor")
            hyena_in.tensor(pe, stream); k.meet(pe, "tensor")
            hyena.tensor_front(pe); k.meet(pe, "tensor")
            hyena.tensor(pe); k.meet(pe, "tensor")
            hyena_norm.tensor(pe); k.meet(pe, "tensor")
            mix_out.tensor(pe, stream); k.meet(pe, "tensor")
            ffn_norm.tensor(pe); k.meet(pe, "tensor")
            router.tensor(pe); k.meet(pe, "tensor")
            experts.tensor(pe); k.meet(pe, "tensor")
            further.tensor(pe); k.meet(pe, "tensor")
            combine.tensor(pe)

        @block.vector
        def _(dve):
            stream, st = Stream(k), Steps(dve, k.sem("vector_steps"))
            setup.vector(dve); k.meet(dve, "vector")
            cond.vector(dve, st); k.meet(dve, "vector")
            din.vector(dve, st, stream); k.meet(dve, "vector")
            qk_norm.vector(dve, st); k.meet(dve, "vector")
            heads.vector(dve, st); k.meet(dve, "vector")
            o_norm.vector(dve, st); k.meet(dve, "vector")
            res0.vector(dve, st, stream); k.meet(dve, "vector")
            up0.vector(dve, st, stream); k.meet(dve, "vector")
            down0.vector(dve, st, stream); k.meet(dve, "vector")
            rin.vector(dve, st, stream); k.meet(dve, "vector")
            reth.vector(dve, st); k.meet(dve, "vector")
            res1.vector(dve, st, stream); k.meet(dve, "vector")
            up1.vector(dve, st, stream); k.meet(dve, "vector")
            down1.vector(dve, st, stream); k.meet(dve, "vector")
            prepend.vector(dve); k.meet(dve, "vector")
            mix_norm.vector(dve, st); k.meet(dve, "vector")
            hgrn_in.vector(dve, stream); k.meet(dve, "vector")
            gates.vector(dve, st); k.meet(dve, "vector")
            hgrn.vector(dve, st); k.meet(dve, "vector")
            hgrn_norm.vector(dve, st); k.meet(dve, "vector")
            hyena_in.vector(dve, stream); k.meet(dve, "vector")
            hyena.vector_front(dve, st); k.meet(dve, "vector")
            hyena.vector(dve, st); k.meet(dve, "vector")
            hyena_norm.vector(dve, st); k.meet(dve, "vector")
            mix_out.vector(dve, stream); k.meet(dve, "vector")
            ffn_norm.vector(dve, st); k.meet(dve, "vector")
            router.vector(dve, st); k.meet(dve, "vector")
            experts.vector(dve); k.meet(dve, "vector")
            further.vector(dve); k.meet(dve, "vector")
            combine.vector(dve, st)

        @block.scalar
        def _(act):
            stream = Stream(k)
            setup.scalar(act); k.meet(act, "scalar")
            cond.scalar(act); k.meet(act, "scalar")
            din.scalar(act, stream); k.meet(act, "scalar")
            qk_norm.scalar(act); k.meet(act, "scalar")
            heads.scalar(act); k.meet(act, "scalar")
            o_norm.scalar(act); k.meet(act, "scalar")
            res0.scalar(act, stream); k.meet(act, "scalar")
            up0.scalar(act, stream); k.meet(act, "scalar")
            down0.scalar(act, stream); k.meet(act, "scalar")
            rin.scalar(act, stream); k.meet(act, "scalar")
            reth.scalar(act); k.meet(act, "scalar")
            res1.scalar(act, stream); k.meet(act, "scalar")
            up1.scalar(act, stream); k.meet(act, "scalar")
            down1.scalar(act, stream); k.meet(act, "scalar")
            prepend.scalar(act); k.meet(act, "scalar")
            mix_norm.scalar(act); k.meet(act, "scalar")
            hgrn_in.scalar(act, stream); k.meet(act, "scalar")
            gates.scalar(act); k.meet(act, "scalar")
            hgrn.scalar(act); k.meet(act, "scalar")
            hgrn_norm.scalar(act); k.meet(act, "scalar")
            hyena_in.scalar(act, stream); k.meet(act, "scalar")
            hyena.scalar_front(act); k.meet(act, "scalar")
            hyena.scalar(act); k.meet(act, "scalar")
            hyena_norm.scalar(act); k.meet(act, "scalar")
            mix_out.scalar(act, stream); k.meet(act, "scalar")
            ffn_norm.scalar(act); k.meet(act, "scalar")
            router.scalar(act); k.meet(act, "scalar")
            experts.scalar(act); k.meet(act, "scalar")
            further.scalar(act); k.meet(act, "scalar")
            combine.scalar(act)

        @block.gpsimd
        def _(pool):
            stream = Stream(k)
            for stage in (setup, cond):
                stage.gpsimd(pool); k.meet(pool, "gpsimd")
            din.gpsimd(pool, stream); k.meet(pool, "gpsimd")
            for stage in (qk_norm, heads):
                stage.gpsimd(pool); k.meet(pool, "gpsimd")
            pool.memset(k.spare[:], 0.0)
            o_norm.gpsimd(pool); k.meet(pool, "gpsimd")
            zero_slots(k, pool)
            for stage in (res0, up0, down0, rin):
                stage.gpsimd(pool, stream); k.meet(pool, "gpsimd")
            reth.gpsimd(pool); k.meet(pool, "gpsimd")
            for stage in (res1, up1, down1):
                stage.gpsimd(pool, stream); k.meet(pool, "gpsimd")
            for stage in (prepend, mix_norm):
                stage.gpsimd(pool); k.meet(pool, "gpsimd")
            hgrn_in.gpsimd(pool, stream); k.meet(pool, "gpsimd")
            for stage in (gates, hgrn, hgrn_norm):
                stage.gpsimd(pool); k.meet(pool, "gpsimd")
            hyena_in.gpsimd(pool, stream); k.meet(pool, "gpsimd")
            k.meet(pool, "gpsimd")
            for stage in (hyena, hyena_norm, mix_out, ffn_norm, router, experts, further):
                stage.gpsimd(pool); k.meet(pool, "gpsimd")
            combine.gpsimd(pool)


def kernel(**inputs):
    import concourse.bacc as bacc
    from concourse.bass_utils import run_bass_kernel_spmd as run

    nc = bacc.Bacc("TRN2", target_bir_lowering=False, num_devices=1)
    arrays, ins = {}, {}
    for name, a in inputs.items():
        if name.startswith(("gmlp", "sb_")):
            continue
        a = np.ascontiguousarray(a)
        shape = a.shape
        ap = nc.dram_tensor("in_" + name, shape, F32, kind="ExternalInput").ap()
        arrays["in_" + name] = a
        flat_names = ("gdn_conv_w", "cond_b", "c", "ada_b", "ln_g", "ln_b", "ffn_conv_b", "conv_w_2", "conv_b_2", "ffn_conv_w",
                      "filt_skip_2", "hyena_norm_2", "hgrn_norm_2", "lb_fwd_2", "lb_bwd_2", "norm_mix_2", "norm_ffn_2", "gdn_norm_w")
        names = "abcde"[:len(shape)]
        if name in flat_names:
            ap = ap.rearrange(f"{' '.join(names)} -> ({' '.join(names)})")
        elif shape[0] == 1 and len(shape) > 1 and name != "c":
            ap = ap[0]
        ins[name] = ap
    tables = {}
    for name, a in shape_tables().items():
        tables[name] = nc.dram_tensor(name, a.shape, F32, kind="ExternalInput").ap()
        arrays[name] = a
    out = nc.dram_tensor("out", (1, T, D), F32, kind="ExternalOutput").ap()
    x_slots = nc.dram_tensor("x_slots", (N_SLOTS, D), F32, kind="Internal").ap()
    y_slots = nc.dram_tensor("y_slots", (N_SLOTS, D), F32, kind="Internal").ap()
    program(nc, ins, tables, out[0], x_slots, y_slots)
    return run(nc, [arrays], core_ids=[0]).results[0]["out"]
```
